# Optimizing a Trainium2 kernel written in Bass

```python
import math
import jax, jax.numpy as jnp
from jax import lax
import numpy as np

D_MODEL = 1024
BATCH = 1
SEQ = 512
DEPTH = 2

GRID_W = 64
CTX_LEN = 256
GDN_DK = 128
GDN_DV = 128
GDN_W = D_MODEL // 2
GDN_HEADS = GDN_W // GDN_DV
FNET_W = D_MODEL // 4
FNET_GROUPS = 4
FNET_GDIM = FNET_W // FNET_GROUPS
CONV_W = D_MODEL // 4
CONV_GROUPS = 4
MIX_W = GDN_W + FNET_W + CONV_W
SHORT_CONV = 3
CONV_K = 31
CHUNK = 64
QKV_OFF = 0
Z_OFF = 3 * GDN_W
A_OFF = Z_OFF + GDN_W
B_OFF = A_OFF + 2 * GDN_HEADS
F_OFF = B_OFF + 2 * GDN_HEADS
C_OFF = F_OFF + FNET_W
IN_W = C_OFF + 2 * CONV_W
PEER_HEADS = 8
PEER_NKEYS = 128
PEER_EXPERTS = PEER_NKEYS * PEER_NKEYS
PEER_TOPK = 16
PEER_DQ = 256
PEER_DH = PEER_DQ // 2
PEER_BLOCK = 128
EPS = 1e-6
NEG = -1e30

kernel_name = "hybrid_gdn_fnet_conformer_peer_dit"

def _rms(x, w):
    xf = x.astype(jnp.float32)
    y = xf * lax.rsqrt(jnp.mean(xf * xf, axis=-1, keepdims=True) + EPS)
    return (y * w.astype(jnp.float32)).astype(x.dtype)

def _l2n(t):
    return t * lax.rsqrt(jnp.sum(t * t, axis=-1, keepdims=True) + EPS)

def _dwconv(x, w, pad):
    return lax.conv_general_dilated(
        x, w[:, None, :].astype(x.dtype), (1,), [(pad, pad)],
        dimension_numbers=("NWC", "WIO", "NWC"), feature_group_count=x.shape[-1])

def _gdn_chunked(q, k, v, g, beta, s0):
    b, h, L, _ = q.shape
    dv = v.shape[-1]
    n = L // CHUNK
    blk = lambda t: t.reshape(b, h, n, CHUNK, *t.shape[3:])
    q, k, v, g, beta = blk(q), blk(k), blk(v), blk(g), blk(beta)
    g = jnp.cumsum(g, axis=-1)
    idx = jnp.arange(CHUNK)
    incl = idx[:, None] >= idx[None, :]
    strict = idx[:, None] > idx[None, :]
    decay = jnp.exp(jnp.where(incl, g[..., :, None] - g[..., None, :], NEG))
    kb = k * beta[..., None]
    a_mat = jnp.where(strict, jnp.einsum("bhnid,bhnjd->bhnij", kb, k) * decay, 0.0)
    rhs = jnp.concatenate([v * beta[..., None], kb * jnp.exp(g)[..., None]], axis=-1)
    sol = lax.linalg.triangular_solve(a_mat + jnp.eye(CHUNK, dtype=jnp.float32), rhs,
                                      left_side=True, lower=True, unit_diagonal=True)
    u, w = sol[..., :dv], sol[..., dv:]
    qk = jnp.einsum("bhnid,bhnjd->bhnij", q, k) * decay
    g_last = g[..., -1]
    k_tail = k * jnp.exp(g_last[..., None] - g)[..., None]
    q_dec = q * jnp.exp(g)[..., None]

    def step(s, inp):
        q_i, k_i, u_i, w_i, qk_i, gl_i = inp
        v_new = u_i - jnp.einsum("bhck,bhkv->bhcv", w_i, s)
        o_i = jnp.einsum("bhck,bhkv->bhcv", q_i, s) + jnp.einsum("bhcj,bhjv->bhcv", qk_i, v_new)
        s = s * jnp.exp(gl_i)[..., None, None] + jnp.einsum("bhck,bhcv->bhkv", k_i, v_new)
        return s, o_i

    mv = lambda t: jnp.moveaxis(t, 2, 0)
    s_fin, o = lax.scan(step, s0, (mv(q_dec), mv(k_tail), mv(u), mv(w), mv(qk), mv(g_last)))
    o = jnp.moveaxis(o, 0, 2).reshape(b, h, L, dv)
    return o, s_fin

def _gdn_bidir(q, k, v, g, beta, s0_f, s0_b):
    o_f, s_f = _gdn_chunked(q, k, v, g[0], beta[0], s0_f)
    fl = lambda t: jnp.flip(t, axis=2)
    o_b, s_b = _gdn_chunked(fl(q), fl(k), fl(v), fl(g[1]), fl(beta[1]), s0_b)
    return o_f + fl(o_b), s_f, s_b

def _gdn_inputs(p, conv_qkv, a_log, dt_bias):
    bsz, L, _ = p.shape
    qkv = jax.nn.silu(_dwconv(p[..., QKV_OFF:Z_OFF], conv_qkv, SHORT_CONV // 2)).astype(jnp.float32)
    heads = lambda t: t.reshape(bsz, L, GDN_HEADS, -1).transpose(0, 2, 1, 3)
    q, k, v = (heads(t) for t in jnp.split(qkv, 3, axis=-1))
    q = _l2n(q) * (GDN_DK ** -0.5)
    k = _l2n(k)
    a = p[..., A_OFF:B_OFF].astype(jnp.float32).reshape(bsz, L, 2, GDN_HEADS)
    bb = p[..., B_OFF:F_OFF].astype(jnp.float32).reshape(bsz, L, 2, GDN_HEADS)
    g = -jnp.exp(a_log.astype(jnp.float32)) * jax.nn.softplus(a + dt_bias.astype(jnp.float32))
    beta = jax.nn.sigmoid(bb)
    return q, k, v, g.transpose(2, 0, 3, 1), beta.transpose(2, 0, 3, 1)

def _gdn_out(o, z, w_norm):
    bsz, _, L, _ = o.shape
    o = o.transpose(0, 2, 1, 3)
    o = o * lax.rsqrt(jnp.mean(o * o, axis=-1, keepdims=True) + EPS) * w_norm.astype(jnp.float32)
    zf = z.astype(jnp.float32).reshape(bsz, L, GDN_HEADS, GDN_DV)
    return (o * jax.nn.silu(zf)).reshape(bsz, L, GDN_W).astype(z.dtype)

def _fnet(f):
    bsz, L, _ = f.shape
    ff = f.astype(jnp.float32).reshape(bsz, L, FNET_GROUPS, FNET_GDIM)
    y = jnp.fft.fft2(ff, axes=(1, 3), norm="ortho").real
    return y.reshape(bsz, L, FNET_W).astype(f.dtype)

def _conv_module(gl, dw_w, dw_b, gn_w, gn_b, rows):
    bsz, L, _ = gl.shape
    y = gl[..., :CONV_W] * jax.nn.sigmoid(gl[..., CONV_W:])
    if rows is not None:
        y = y.reshape(bsz * rows, GRID_W, CONV_W)
    y = (_dwconv(y, dw_w, CONV_K // 2) + dw_b.astype(y.dtype)).reshape(bsz, L, CONV_W)
    yf = y.astype(jnp.float32).reshape(bsz, L, CONV_GROUPS, CONV_W // CONV_GROUPS)
    mu = jnp.mean(yf, axis=-1, keepdims=True)
    var = jnp.mean(jnp.square(yf - mu), axis=-1, keepdims=True)
    yf = ((yf - mu) * lax.rsqrt(var + EPS)).reshape(bsz, L, CONV_W)
    yf = yf * gn_w.astype(jnp.float32) + gn_b.astype(jnp.float32)
    return jax.nn.silu(yf).astype(gl.dtype)

def _mix_out(p, o, gdn_norm, dw_w, dw_b, gn_w, gn_b, w_out, rows):
    y_gdn = _gdn_out(o, p[..., Z_OFF:A_OFF], gdn_norm)
    y_f = _fnet(p[..., F_OFF:C_OFF])
    y_c = _conv_module(p[..., C_OFF:IN_W], dw_w, dw_b, gn_w, gn_b, rows)
    return jnp.concatenate([y_gdn, y_f, y_c], axis=-1) @ w_out

def _peer(h, wq, keys, u_tab, v_tab):
    bsz, L, D = h.shape
    T = bsz * L
    hf = h.reshape(T, D)
    qr = (hf @ wq).reshape(T, PEER_HEADS, 2, PEER_DH)
    s = jnp.einsum("thpd,hpkd->thpk", qr, keys).astype(jnp.float32)
    sv, si = lax.top_k(s, PEER_TOPK)
    cand = (sv[:, :, 0, :, None] + sv[:, :, 1, None, :]).reshape(T, PEER_HEADS, -1)
    cid = (si[:, :, 0, :, None] * PEER_NKEYS + si[:, :, 1, None, :]).reshape(T, PEER_HEADS, -1)
    fv, fi = lax.top_k(cand, PEER_TOPK)
    eid = jnp.take_along_axis(cid, fi, axis=-1).reshape(T, -1)
    gw = jax.nn.softmax(fv, axis=-1).astype(h.dtype).reshape(T, -1)
    nb = T // PEER_BLOCK

    def blk(args):
        hb, eb, gb = args
        act = jax.nn.gelu(jnp.einsum("tkd,td->tk", u_tab[eb], hb))
        return jnp.einsum("tk,tkd->td", gb * act, v_tab[eb])

    out = lax.map(blk, (hf.reshape(nb, PEER_BLOCK, D),
                        eid.reshape(nb, PEER_BLOCK, -1),
                        gw.reshape(nb, PEER_BLOCK, -1)))
    return out.reshape(bsz, L, D)

def _layer(x, xc, mod, mod_c, rows, last, norm1, norm2, w_in, conv_qkv, a_log, dt_bias,
           gdn_norm, dw_w, dw_b, gn_w, gn_b, w_out, peer_wq, peer_keys, peer_u, peer_v):
    sh1, sc1, gt1, sh2, sc2, gt2 = (mod[:, j][:, None, :] for j in range(6))
    csh1, csc1, cgt1, csh2, csc2, cgt2 = (mod_c[j] for j in range(6))
    h = _rms(x, norm1) * (1 + sc1) + sh1
    hc = _rms(xc, norm1) * (1 + csc1) + csh1
    p = h @ w_in
    pc = hc @ w_in
    zero = jnp.zeros((x.shape[0], GDN_HEADS, GDN_DK, GDN_DV), jnp.float32)
    oc, s_f, s_b = _gdn_bidir(*_gdn_inputs(pc, conv_qkv, a_log, dt_bias), zero, zero)
    o, _, _ = _gdn_bidir(*_gdn_inputs(p, conv_qkv, a_log, dt_bias), s_f, s_b)
    mix = lambda pp, oo, r: _mix_out(pp, oo, gdn_norm, dw_w, dw_b, gn_w, gn_b, w_out, r)
    peer = lambda hh: _peer(hh, peer_wq, peer_keys, peer_u, peer_v)
    x = x + gt1 * mix(p, o, rows)
    x = x + gt2 * peer(_rms(x, norm2) * (1 + sc2) + sh2)
    if not last:
        xc = xc + cgt1 * mix(pc, oc, None)
        xc = xc + cgt2 * peer(_rms(xc, norm2) * (1 + csc2) + csh2)
    return x, xc

def setup_inputs(seed: int = 0) -> dict:
    key = jax.random.key(seed)
    ks = jax.random.split(key, 24)
    D = D_MODEL
    nrm = lambda k, shape, s: jax.random.normal(k, shape, jnp.float32) * s
    dt = jnp.exp(jax.random.uniform(ks[11], (DEPTH, 2, GDN_HEADS), jnp.float32,
                                    math.log(1e-3), math.log(1e-1)))
    return {
        "x": nrm(ks[0], (BATCH, SEQ, D), 1.0),
        "c": nrm(ks[1], (BATCH, D), 1.0),
        "ctx": nrm(ks[2], (BATCH, CTX_LEN, D), 1.0),
        "c_ctx": nrm(ks[3], (D,), 1.0),
        "w_mod": nrm(ks[4], (DEPTH, D, 6 * D), 0.5 * D ** -0.5),
        "b_mod": nrm(ks[5], (DEPTH, 6 * D), 0.01),
        "norm1": 1.0 + nrm(ks[6], (DEPTH, D), 0.02),
        "norm2": 1.0 + nrm(ks[7], (DEPTH, D), 0.02),
        "w_in": nrm(ks[8], (DEPTH, D, IN_W), D ** -0.5),
        "conv_qkv": nrm(ks[9], (DEPTH, SHORT_CONV, 3 * GDN_W), SHORT_CONV ** -0.5),
        "a_log": jnp.log(jax.random.uniform(ks[10], (DEPTH, 2, GDN_HEADS), jnp.float32, 1.0, 16.0)),
        "dt_bias": dt + jnp.log(-jnp.expm1(-dt)),
        "gdn_norm": 1.0 + nrm(ks[12], (DEPTH, GDN_DV), 0.02),
        "dw_w": nrm(ks[13], (DEPTH, CONV_K, CONV_W), CONV_K ** -0.5),
        "dw_b": nrm(ks[14], (DEPTH, CONV_W), 0.02),
        "gn_w": 1.0 + nrm(ks[15], (DEPTH, CONV_W), 0.02),
        "gn_b": nrm(ks[16], (DEPTH, CONV_W), 0.02),
        "w_out": nrm(ks[17], (DEPTH, MIX_W, D), MIX_W ** -0.5),
        "peer_wq": nrm(ks[18], (DEPTH, D, PEER_HEADS * PEER_DQ), D ** -0.5),
        "peer_keys": nrm(ks[19], (DEPTH, PEER_HEADS, 2, PEER_NKEYS, PEER_DH), PEER_DH ** -0.5),
        "peer_u": nrm(ks[20], (DEPTH, PEER_EXPERTS, D), D ** -0.5),
        "peer_v": nrm(ks[21], (DEPTH, PEER_EXPERTS, D), 1.0),
        "final_norm": 1.0 + nrm(ks[22], (D,), 0.02),
    }

def reference(x, c, ctx, c_ctx, w_mod, b_mod, norm1, norm2, w_in, conv_qkv, a_log, dt_bias,
              gdn_norm, dw_w, dw_b, gn_w, gn_b, w_out, peer_wq, peer_keys, peer_u, peer_v,
              final_norm):
    rows = x.shape[1] // GRID_W
    xc = ctx
    for i in range(DEPTH):
        mod = (jax.nn.silu(c) @ w_mod[i] + b_mod[i]).reshape(c.shape[0], 6, D_MODEL)
        mod_c = (jax.nn.silu(c_ctx) @ w_mod[i] + b_mod[i]).reshape(6, D_MODEL)
        x, xc = _layer(x, xc, mod, mod_c, rows, i == DEPTH - 1,
                       norm1[i], norm2[i], w_in[i], conv_qkv[i], a_log[i], dt_bias[i],
                       gdn_norm[i], dw_w[i], dw_b[i], gn_w[i], gn_b[i], w_out[i],
                       peer_wq[i], peer_keys[i], peer_u[i], peer_v[i])
    return _rms(x, final_norm)


_drawn_inputs = setup_inputs


def setup_inputs(seed=0):
    import zlib

    import numpy as np

    out = dict(_drawn_inputs(seed))
    spreads = {}
    factors = {'c_ctx': 2.688,
     'gdn_norm': 3.255,
     'dw_b': 2.849,
     'gn_w': 3.179,
     'gn_b': 3.343,
     'final_norm': 2.821}
    for name, (base, spread) in spreads.items():
        noise = np.random.default_rng([zlib.crc32(name.encode()), seed]).standard_normal(out[name].shape)
        drawn = base * np.exp(spread * noise) if base else spread * noise
        out[name] = __import__('jax').numpy.asarray(drawn.astype(out[name].dtype))
    for name, factor in factors.items():
        out[name] = (out[name] * factor).astype(out[name].dtype)
    return out
```

```python
import concourse.bass as bass
from concourse import mybir
from contextlib import ExitStack, contextmanager

FP32 = mybir.dt.float32
U32 = mybir.dt.uint32
ALU = mybir.AluOpType
ACT = mybir.ActivationFunctionType
AXX = mybir.AxisListType.X

P = 128
D = 1024
KD = D // P
SEQ, CTX = 512, 256
T = SEQ + CTX
NT = T // P
NC = CTX // P
DEPTH = 2
GRID_W = 64
H = 4
GW = H * P
CHUNK = 64
IN_W = 4 * GW + 4 * H + 256 + 512
Z_OFF, A_OFF = 3 * GW, 4 * GW
F_OFF = A_OFF + 4 * H
C_OFF = F_OFF + 256
NQKV = 3 * GW // P
TAPS, CONV_K = 3, 31
HALO = CONV_K // 2
PH, NKEYS, TOPK = 8, 128, 16
HP = 2 * PH
SLOTS = PH * TOPK
EPS = 1e-6
LEVELS = [1, 2, 4, 8, 16, 32]
NEG = -3.0e38

CONSTS = (["ident", "L0", "L1", "M0", "M1", "CH0", "CH1", "ones", "gmean", "C64", "S64"]
          + [f"B{d}_{n}" for d in range(2) for n in range(len(LEVELS))])
PRM = {"conv": 0, "dw": TAPS * NQKV, "dwb": TAPS * NQKV + 2 * CONV_K}
PRM["gnw"] = PRM["dwb"] + 2
PRM["gnb"] = PRM["gnw"] + 2
NPRM = PRM["gnb"] + 2


class Kit:

    def c(self, name):
        at = CONSTS.index(name) * P
        return self.cst[:, at:at + P]

    def c2(self, name):
        at = CONSTS.index(name) * P
        return self.cst[:, at:at + 2 * P]


@contextmanager
def phase(nc, kit, *names, gathers=0):
    with ExitStack() as st:
        kit.phases += 1
        sems = [st.enter_context(nc.semaphore(f"{n}_{kit.phases}")) for n in names]
        yield sems
        for s in sems[:gathers]:
            nc.gpsimd.dma_reset(range(s.num, s.num + 1))
            nc.gpsimd.sem_clear(s)
        for s in sems[gathers:]:
            nc.sync.sem_clear(s)
        nc.all_engine_barrier()


def linker(eng, sem):
    count = [0]

    def link(ins):
        count[0] += 1
        ins.then_inc(sem, 1)
        eng.wait_ge(sem, count[0])

    return link


def setup(nc, kit):
    with phase(nc, kit, "const_in", "x_in") as (const_in, x_in):
        with nc.Block() as block:
            @block.sync
            def _(sp):
                sp.dma_start(kit.cst[:], kit.consts).then_inc(const_in, 16)
                sp.dma_start(kit.x_d[0:CTX, :], kit.ctx[0, :, :]).then_inc(x_in, 16)
                sp.dma_start(kit.x_d[CTX:T, :], kit.x[0, :, :]).then_inc(x_in, 16)
                sp.wait_ge(const_in, 16)
                sp.wait_ge(x_in, 32)

            @block.vector
            def _(dve):
                nc.vector.memset(kit.eps[:, 0:1], EPS)
                nc.vector.memset(kit.eps[:, 1:2], EPS * P)


def modulation(nc, kit, L):
    NCOL = 512
    NB = 6 * D // NCOL
    RING = 3
    with ExitStack() as mem, phase(nc, kit, "cond_in", "bias_in", "prm_in", "w0", "w1", "w2", "turned",
                                   "cond_ready", "prod_ready", "row_ready", "stored") as (
            cond_in, bias_in, prm_in, w0, w1, w2, turned, cond_ready, prod_ready, row_ready, stored):
        w_in = [w0, w1, w2]
        sb = lambda n, s: mem.enter_context(nc.sbuf_tensor(f"{n}_{L}", s, FP32))
        cond = sb("cond", [16, P])
        prm_rows = sb("prm_rows", [NPRM, P])
        condT = sb("condT", [P, KD, 2])
        wm = sb("wm", [P, RING, KD, NCOL])
        row = sb("modrow", [2, 6 * D])
        ps = kit.ps
        ident = kit.c("ident")

        with nc.Block() as block:
            @block.sync
            def _(sp):
                sp.dma_start(cond[0:8, :], kit.c_ctx.rearrange("(k p) -> k p", p=P)).then_inc(cond_in, 16)
                sp.dma_start(cond[8:16, :], kit.cnd[0, :].rearrange("(k p) -> k p", p=P)).then_inc(cond_in, 16)
                for i in range(2):
                    sp.dma_start(row[i:i + 1, :], kit.b_mod[L:L + 1, :]).then_inc(bias_in, 16)
                rows = [("conv", kit.conv_qkv[L].rearrange("t (c p) -> (t c) p", p=P), TAPS * NQKV),
                        ("dw", kit.dw_w[L].rearrange("t (c p) -> (t c) p", p=P), 2 * CONV_K),
                        ("dwb", kit.dw_b[L].rearrange("(c p) -> c p", p=P), 2),
                        ("gnw", kit.gn_w[L].rearrange("(c p) -> c p", p=P), 2),
                        ("gnb", kit.gn_b[L].rearrange("(c p) -> c p", p=P), 2)]
                for name, src, n in rows:
                    sp.dma_start(prm_rows[PRM[name]:PRM[name] + n, :], src).then_inc(prm_in, 16)
                for n in range(NB):
                    if n >= RING:
                        sp.wait_ge(prod_ready, n - RING + 1)
                    sp.dma_start(wm[:, n % RING, :, :],
                                 kit.w_mod[L, :, n * NCOL:(n + 1) * NCOL].rearrange("(k p) n -> p k n", p=P)
                                 ).then_inc(w_in[n % RING], 16)
                sp.wait_ge(row_ready, NB)
                sp.dma_start(kit.mod_d, row[:, :]).then_inc(stored, 16)
                sp.wait_ge(stored, 16)

            @block.tensor
            def _(pe):
                pe.wait_ge(cond_in, 32)
                nc.tensor.transpose(ps[:, 0, 0:16], cond[:, :], ident[0:16, 0:16]).then_inc(turned, 1)
                pe.wait_ge(prm_in, 80)
                nc.tensor.transpose(ps[:, 1, 0:NPRM], prm_rows[:, :], ident[0:NPRM, 0:NPRM]).then_inc(turned, 1)
                pe.wait_ge(cond_ready, 1)
                for n in range(NB):
                    pe.wait_ge(w_in[n % RING], 16 * (n // RING + 1))
                    if n >= 4:
                        pe.wait_ge(row_ready, n - 3)
                    for k in range(KD):
                        last = nc.tensor.matmul(ps[0:2, 2 + n % 4, 0:NCOL], condT[:, k, :], wm[:, n % RING, k, :],
                                                start=k == 0, stop=k == KD - 1)
                    last.then_inc(prod_ready, 1)

            @block.scalar
            def _(act):
                act.wait_ge(turned, 1)
                nc.scalar.activation(condT[:, :, :].rearrange("p k s -> p s k"),
                                     ps[:, 0, 0:16].rearrange("p (s k) -> p s k", s=2), ACT.Silu
                                     ).then_inc(cond_ready, 1)

            @block.vector
            def _(dve):
                dve.wait_ge(turned, 2)
                nc.vector.tensor_copy(kit.prm[:, :], ps[:, 1, 0:NPRM])
                dve.wait_ge(bias_in, 32)
                for n in range(NB):
                    dve.wait_ge(prod_ready, n + 1)
                    part = row[:, n * NCOL:(n + 1) * NCOL]
                    nc.vector.tensor_tensor(part, part, ps[0:2, 2 + n % 4, 0:NCOL], ALU.add).then_inc(row_ready, 1)


def mod_row(kit, stream, j):
    return kit.mod_d[stream:stream + 1, j * D:(j + 1) * D].broadcast_to([P, D])


def norm_in(nc, kit, L, hT):
    with ExitStack() as mem, phase(nc, kit, "rows_in", "x0", "x1", "scale_ready", "ss_ready", "ms_ready",
                                   "root_ready", "h_ready", "turned", "hT_ready", "dve_step") as (
            rows_in, x0, x1, scale_ready, ss_ready, ms_ready, root_ready, h_ready, turned, hT_ready, dve_step):
        x_in = [x0, x1]
        sb = lambda n, s: mem.enter_context(nc.sbuf_tensor(f"n1{n}_{L}", s, FP32))
        gain = sb("gain", [P, D])
        sc = sb("sc", [P, 2, D])
        sh = sb("sh", [P, 2, D])
        xb = sb("x", [P, 2, D])
        hb = sb("h", [P, 2, D])
        sq = sb("sq", [P, D])
        ss = sb("ss", [P, 3, NT])
        ps = kit.ps
        ident = kit.c("ident")

        with nc.Block() as block:
            @block.sync
            def _(sp):
                sp.dma_start(gain[:], kit.norm1[L:L + 1, :].broadcast_to([P, D])).then_inc(rows_in, 16)
                for s in range(2):
                    sp.dma_start(sc[:, s, :], mod_row(kit, s, 1)).then_inc(rows_in, 16)
                    sp.dma_start(sh[:, s, :], mod_row(kit, s, 0)).then_inc(rows_in, 16)
                for t in range(NT):
                    if t >= 2:
                        sp.wait_ge(h_ready, t - 1)
                    sp.dma_start(xb[:, t % 2, :], kit.x_d[t * P:(t + 1) * P, :]).then_inc(x_in[t % 2], 16)

            @block.scalar
            def _(act):
                for t in range(NT):
                    act.wait_ge(x_in[t % 2], 16 * (t // 2 + 1))
                    if t:
                        act.wait_ge(ss_ready, t)
                    nc.scalar.activation(sq[:], xb[:, t % 2, :], ACT.Square, accum_out=ss[:, 0, t:t + 1]
                                         ).then_inc(ss_ready, 1)
                    act.wait_ge(ms_ready, t + 1)
                    nc.scalar.activation(ss[:, 2, t:t + 1], ss[:, 1, t:t + 1], ACT.Sqrt).then_inc(root_ready, 1)
                    act.wait_ge(turned, t + 1)
                    b = 2 * (t % 2)
                    nc.scalar.activation(hT[:, :, t * P:(t + 1) * P],
                                         ps[:, b:b + 2, :].rearrange("p b (k n) -> p (b k) n", n=P),
                                         ACT.Copy).then_inc(hT_ready, 1)

            @block.vector
            def _(dve):
                link = linker(dve, dve_step)
                dve.wait_ge(rows_in, 80)
                for s in range(2):
                    link(nc.vector.scalar_tensor_tensor(out=sc[:, s, :], in0=sc[:, s, :], scalar=1.0,
                                                        in1=gain[:], op0=ALU.add, op1=ALU.mult))
                for t in range(NT):
                    s = int(t >= NC)
                    dve.wait_ge(ss_ready, t + 1)
                    nc.vector.tensor_scalar(ss[:, 1, t:t + 1], ss[:, 0, t:t + 1], 1.0 / D, EPS,
                                            ALU.mult, ALU.add).then_inc(ms_ready, 1)
                    dve.wait_ge(root_ready, t + 1)
                    link(nc.vector.reciprocal(ss[:, 0, t:t + 1], ss[:, 2, t:t + 1]))
                    if t >= 2:
                        dve.wait_ge(turned, t - 1)
                    link(nc.vector.scalar_tensor_tensor(out=hb[:, t % 2, :], in0=xb[:, t % 2, :],
                                                        scalar=ss[:, 0, t:t + 1], in1=sc[:, s, :],
                                                        op0=ALU.mult, op1=ALU.mult))
                    nc.vector.tensor_tensor(hb[:, t % 2, :], hb[:, t % 2, :], sh[:, s, :], ALU.add
                                            ).then_inc(h_ready, 1)

            @block.tensor
            def _(pe):
                for t in range(NT):
                    pe.wait_ge(h_ready, t + 1)
                    if t >= 2:
                        pe.wait_ge(hT_ready, t - 1)
                    for k in range(KD):
                        last = nc.tensor.transpose(ps[:, 2 * (t % 2) + k // 4, (k % 4) * P:(k % 4 + 1) * P],
                                                   hb[:, t % 2, k * P:(k + 1) * P], ident)
                    last.then_inc(turned, 1)


def projection(nc, kit, L, hT, qkvT, zs, ab, fT, aT, gT):
    chunks = ([c * P for c in range(NQKV)] + [F_OFF + c * P for c in range(2)] + [C_OFF + c * P for c in range(4)])
    RING = 3
    NF = len(chunks)
    with ExitStack() as mem, phase(nc, kit, "w0", "w1", "w2", "wz_in", "proj_ready", "proj_read", "p_ready",
                                   "y_ready", "y_used", "rows_ready", "dve_step") as (
            w0, w1, w2, wz_in, proj_ready, proj_read, p_ready, y_ready, y_used, rows_ready, dve_step):
        w_in = [w0, w1, w2]
        sb = lambda n, s: mem.enter_context(nc.sbuf_tensor(f"pj{n}_{L}", s, FP32))
        w = sb("w", [P, RING, KD, P])
        wz = sb("wz", [P, KD, GW])
        wab = sb("wab", [P, KD, 4 * H])
        pT = sb("p", [P, 2, T])
        yT = sb("y", [P, 2, T])
        ps = kit.ps
        w_d = kit.w_in[L].rearrange("(k p) n -> p k n", p=P)

        with nc.Block() as block:
            @block.sync
            def _(sp):
                for c, off in enumerate(chunks):
                    if c >= RING:
                        sp.wait_ge(proj_ready, c - RING + 1)
                    sp.dma_start(w[:, c % RING, :, :], w_d[:, :, off:off + P]).then_inc(w_in[c % RING], 16)
                    if c == RING:
                        sp.dma_start(wz[:], w_d[:, :, Z_OFF:A_OFF]).then_inc(wz_in, 16)
                        sp.dma_start(wab[:], w_d[:, :, A_OFF:F_OFF]).then_inc(wz_in, 16)

            @block.tensor
            def _(pe):
                for c in range(NF):
                    pe.wait_ge(w_in[c % RING], 16 * (c // RING + 1))
                    if c >= 2:
                        pe.wait_ge(proj_read, c - 1)
                    b = 2 * (c % 2)
                    for k in range(KD):
                        nc.tensor.matmul(ps[:, b, 0:SEQ], w[:, c % RING, k, :], hT[:, k, CTX:T],
                                         start=k == 0, stop=k == KD - 1)
                    for k in range(KD):
                        last = nc.tensor.matmul(ps[:, b + 1, 0:CTX], w[:, c % RING, k, :], hT[:, k, 0:CTX],
                                                start=k == 0, stop=k == KD - 1)
                    last.then_inc(proj_ready, 1)
                pe.wait_ge(wz_in, 32)
                for t in range(NT):
                    if t >= 2:
                        pe.wait_ge(rows_ready, t - 1)
                    for k in range(KD):
                        nc.tensor.matmul(ps[:, 4 + 2 * (t % 2), 0:GW], hT[:, k, t * P:(t + 1) * P], wz[:, k, :],
                                         start=k == 0, stop=k == KD - 1)
                    for k in range(KD):
                        last = nc.tensor.matmul(ps[:, 5 + 2 * (t % 2), 0:4 * H], hT[:, k, t * P:(t + 1) * P],
                                                wab[:, k, :], start=k == 0, stop=k == KD - 1)
                    last.then_inc(proj_ready, 1)

            @block.scalar
            def _(act):
                def evacuate(c, out, func):
                    act.wait_ge(proj_ready, c + 1)
                    b = 2 * (c % 2)
                    nc.scalar.activation(out[:, CTX:T], ps[:, b, 0:SEQ], func)
                    return nc.scalar.activation(out[:, 0:CTX], ps[:, b + 1, 0:CTX], func)

                def silu(c):
                    act.wait_ge(y_ready, c + 1)
                    nc.scalar.activation(qkvT[:, c, :], yT[:, c % 2, :], ACT.Silu).then_inc(y_used, 1)

                for c in range(NQKV):
                    if c >= 2:
                        act.wait_ge(y_ready, c - 1)
                    evacuate(c, pT[:, c % 2, :], ACT.Copy).then_inc(proj_read, 1)
                    if c >= 1:
                        silu(c - 1)
                silu(NQKV - 1)
                for i in range(2):
                    evacuate(NQKV + i, fT[:, i, :], ACT.Copy).then_inc(proj_read, 1)
                for i in range(2):
                    evacuate(NQKV + 2 + i, aT[:, i, :], ACT.Copy).then_inc(proj_read, 1)
                for i in range(2):
                    evacuate(NQKV + 4 + i, gT[:, i, :], ACT.Sigmoid).then_inc(proj_read, 1)
                for t in range(NT):
                    act.wait_ge(proj_ready, NF + t + 1)
                    nc.scalar.activation(zs[:, t, :], ps[:, 4 + 2 * (t % 2), 0:GW], ACT.Silu)
                    nc.scalar.activation(ab[:, t, :], ps[:, 5 + 2 * (t % 2), 0:4 * H], ACT.Copy
                                         ).then_inc(rows_ready, 1)

            @block.vector
            def _(dve):
                link = linker(dve, dve_step)
                for c in range(NQKV):
                    tap = lambda j: kit.prm[:, PRM["conv"] + j * NQKV + c:PRM["conv"] + j * NQKV + c + 1]
                    p, y = pT[:, c % 2, :], yT[:, c % 2, :]
                    dve.wait_ge(proj_read, c + 1)
                    if c >= 2:
                        dve.wait_ge(y_used, c - 1)
                    link(nc.vector.tensor_scalar(y, p, tap(1), None, ALU.mult))
                    for a, b in ((0, CTX), (CTX, T)):
                        link(nc.vector.scalar_tensor_tensor(out=y[:, a + 1:b], in0=p[:, a:b - 1], scalar=tap(0),
                                                            in1=y[:, a + 1:b], op0=ALU.mult, op1=ALU.add))
                    for a, b in ((0, CTX), (CTX, T)):
                        last = nc.vector.scalar_tensor_tensor(out=y[:, a:b - 1], in0=p[:, a + 1:b], scalar=tap(2),
                                                              in1=y[:, a:b - 1], op0=ALU.mult, op1=ALU.add)
                        if a == 0:
                            link(last)
                    last.then_inc(y_ready, 1)


def unit_and_gates(nc, kit, L, qkvT, ab, gate):
    G = 2 * H
    N2 = 2 * H
    with ExitStack() as mem, phase(nc, kit, "rows_in", "sq_ready", "sum_ready", "root_ready", "unit_ready",
                                   "e_alog", "arg_ready", "exp_ready", "dve_step") as (
            rows_in, sq_ready, sum_ready, root_ready, unit_ready, e_alog, arg_ready, exp_ready, dve_step):
        sb = lambda n, s: mem.enter_context(nc.sbuf_tensor(f"un{n}_{L}", s, FP32))
        alog = sb("alog", [P, G])
        dt = sb("dt", [P, G])
        sq = sb("sq", [P, 2, T])
        root = sb("root", [P, 2, T])
        v = sb("v", [P, 8, NT, G])
        ps = kit.ps
        ones = kit.c("ones")

        with nc.Block() as block:
            @block.sync
            def _(sp):
                sp.dma_start(alog[:], kit.a_log[L:L + 1].rearrange("l d h -> l (d h)").broadcast_to([P, G])
                             ).then_inc(rows_in, 16)
                sp.dma_start(dt[:], kit.dt_bias[L:L + 1].rearrange("l d h -> l (d h)").broadcast_to([P, G])
                             ).then_inc(rows_in, 16)

            @block.scalar
            def _(act):
                act.wait_ge(rows_in, 32)
                nc.scalar.activation(alog[:], alog[:], ACT.Exp).then_inc(e_alog, 1)
                act.wait_ge(arg_ready, 1)
                nc.scalar.activation(v[:, 2], v[:, 1], ACT.Exp, scale=-1.0).then_inc(exp_ready, 1)
                nc.scalar.activation(gate[:, :, G:2 * G], ab[:, :, G:2 * G], ACT.Sigmoid).then_inc(exp_ready, 1)
                for c in range(N2 + 1):
                    if c < N2:
                        if c >= 2:
                            act.wait_ge(sum_ready, c - 1)
                        nc.scalar.activation(sq[:, c % 2, :], qkvT[:, c, :], ACT.Square).then_inc(sq_ready, 1)
                    if c >= 1:
                        d = c - 1
                        act.wait_ge(sum_ready, d + 1)
                        if d >= 2:
                            act.wait_ge(unit_ready, d - 1)
                        scale, eps = (float(P), kit.eps[:, 1:2]) if d < H else (1.0, kit.eps[:, 0:1])
                        b = 2 * (d % 2)
                        nc.scalar.activation(root[:, d % 2, 0:512], ps[:, b, :], ACT.Sqrt, bias=eps, scale=scale)
                        nc.scalar.activation(root[:, d % 2, 512:T], ps[:, b + 1, 0:T - 512], ACT.Sqrt, bias=eps,
                                             scale=scale).then_inc(root_ready, 1)

            @block.tensor
            def _(pe):
                for c in range(N2):
                    pe.wait_ge(sq_ready, c + 1)
                    if c >= 2:
                        pe.wait_ge(root_ready, c - 1)
                    b = 2 * (c % 2)
                    nc.tensor.matmul(ps[:, b, :], ones, sq[:, c % 2, 0:512], start=True, stop=True)
                    nc.tensor.matmul(ps[:, b + 1, 0:T - 512], ones, sq[:, c % 2, 512:T], start=True, stop=True
                                     ).then_inc(sum_ready, 1)

            @block.vector
            def _(dve):
                link = linker(dve, dve_step)
                wide = lambda a: a[:, None, :].to_broadcast([P, NT, G])
                dve.wait_ge(rows_in, 32)
                link(nc.vector.tensor_tensor(v[:, 0], ab[:, :, 0:G], wide(dt[:]), ALU.add))
                link(nc.vector.tensor_scalar(v[:, 3], v[:, 0], -1.0, None, ALU.mult))
                nc.vector.tensor_tensor(v[:, 1], v[:, 0], v[:, 3], ALU.max).then_inc(arg_ready, 1)
                dve.wait_ge(exp_ready, 2)
                link(nc.vector.tensor_scalar(v[:, 3], v[:, 2], 2.0, None, ALU.add))
                link(nc.vector.reciprocal(v[:, 4], v[:, 3]))
                link(nc.vector.tensor_tensor(v[:, 5], v[:, 2], v[:, 4], ALU.mult))
                link(nc.vector.tensor_tensor(v[:, 6], v[:, 5], v[:, 5], ALU.mult))
                link(nc.vector.tensor_scalar(v[:, 7], v[:, 6], 1.0 / 17, 1.0 / 15, ALU.mult, ALU.add))
                for n in (13, 11, 9, 7, 5, 3, 1):
                    link(nc.vector.tensor_tensor(v[:, 7], v[:, 7], v[:, 6], ALU.mult))
                    link(nc.vector.tensor_scalar(v[:, 7], v[:, 7], 1.0 / n, None, ALU.add))
                link(nc.vector.scalar_tensor_tensor(out=v[:, 7], in0=v[:, 7], scalar=2.0, in1=v[:, 5],
                                                    op0=ALU.mult, op1=ALU.mult))
                link(nc.vector.scalar_tensor_tensor(out=v[:, 7], in0=v[:, 0], scalar=0.0, in1=v[:, 7],
                                                    op0=ALU.max, op1=ALU.add))
                dve.wait_ge(e_alog, 1)
                nc.vector.scalar_tensor_tensor(out=gate[:, :, 0:G], in0=v[:, 7], scalar=-1.0, in1=wide(alog[:]),
                                               op0=ALU.mult, op1=ALU.mult)
                for c in range(N2):
                    dve.wait_ge(root_ready, c + 1)
                    link(nc.vector.reciprocal(root[:, c % 2, :], root[:, c % 2, :]))
                    nc.vector.tensor_tensor(qkvT[:, c, :], qkvT[:, c, :], root[:, c % 2, :], ALU.mult
                                            ).then_inc(unit_ready, 1)


def conv_and_fnet(nc, kit, L, fT, aT, gT, mixT):
    ROWS = SEQ // GRID_W
    W = GRID_W + 2 * HALO
    segs = [(CTX, SEQ, 4, 0), (0, CTX, 2, 1)]
    with ExitStack() as mem, phase(nc, kit, "dft_in", "pad0", "pad1", "conv0", "conv1", "mean_ready",
                                   "cent_ready", "sq_ready", "var_ready", "root_ready", "norm_ready",
                                   "half_ready", "half_read", "seq_ready", "dve_step", "pool_step") as (
            dft_in, pad0, pad1, conv0, conv1, mean_ready, cent_ready, sq_ready, var_ready, root_ready,
            norm_ready, half_ready, half_read, seq_ready, dve_step, pool_step):
        padded, convolved = [pad0, pad1], [conv0, conv1]
        sb = lambda n, s: mem.enter_context(nc.sbuf_tensor(f"cf{n}_{L}", s, FP32))
        lat = sb("lat", [P, 2, ROWS, W])
        ctx = sb("ctx", [P, 2, CTX + 2 * HALO])
        acc = sb("acc", [P, 2, T])
        sq = sb("sq", [P, 2, T])
        dft_l = sb("dftl", [P, 4, 2, SEQ])
        dft_c = sb("dftc", [P, 2, 2, CTX])
        half = sb("half", [P, NT, 2, 2, P])
        tmp = sb("tmp", [P, SEQ])
        ps = kit.ps
        tables = [dft_l, dft_c]

        def dwconv(eng, link, c):
            link(eng.memset(lat[:, c], 0.0))
            link(eng.memset(ctx[:, c], 0.0))
            link(eng.tensor_tensor(lat[:, c, :, HALO:HALO + GRID_W],
                                   aT[:, c, CTX:T].rearrange("p (r w) -> p r w", w=GRID_W),
                                   gT[:, c, CTX:T].rearrange("p (r w) -> p r w", w=GRID_W), ALU.mult))
            link(eng.tensor_tensor(ctx[:, c, HALO:HALO + CTX], aT[:, c, 0:CTX], gT[:, c, 0:CTX], ALU.mult))
            a_lat = acc[:, c, CTX:T].rearrange("p (r w) -> p r w", w=GRID_W)
            a_ctx = acc[:, c, 0:CTX]
            bias = kit.prm[:, PRM["dwb"] + c:PRM["dwb"] + c + 1]
            for j in range(CONV_K):
                tap = kit.prm[:, PRM["dw"] + 2 * j + c:PRM["dw"] + 2 * j + c + 1]
                for out, src in ((a_lat, lat[:, c, :, j:j + GRID_W]), (a_ctx, ctx[:, c, j:j + CTX])):
                    if j == 0:
                        op = eng.tensor_scalar(out, src, tap, bias, ALU.mult, ALU.add)
                    else:
                        op = eng.scalar_tensor_tensor(out=out, in0=src, scalar=tap, in1=out,
                                                      op0=ALU.mult, op1=ALU.add)
                    if j < CONV_K - 1:
                        link(op)
                    else:
                        op.then_inc(convolved[c], 1)

        with nc.Block() as block:
            @block.sync
            def _(sp):
                for s in range(2):
                    sp.dma_start(dft_l[:, :, s, :], kit.dft_l[s].rearrange("(t p) n -> p t n", p=P)
                                 ).then_inc(dft_in, 16)
                    sp.dma_start(dft_c[:, :, s, :], kit.dft_c[s].rearrange("(t p) n -> p t n", p=P)
                                 ).then_inc(dft_in, 16)

            @block.vector
            def _(dve):
                link = linker(dve, dve_step)
                for c in range(2):
                    dwconv(nc.vector, link, c)
                for c in range(2):
                    dve.wait_ge(mean_ready, c + 1)
                    nc.vector.tensor_tensor(acc[:, c, 0:512], acc[:, c, 0:512], ps[:, 0, :], ALU.subtract
                                            ).then_inc(cent_ready, 1)
                    nc.vector.tensor_tensor(acc[:, c, 512:T], acc[:, c, 512:T], ps[:, 1, 0:T - 512],
                                            ALU.subtract).then_inc(cent_ready, 1)
                    dve.wait_ge(root_ready, c + 1)
                    link(nc.vector.reciprocal(sq[:, c, :], sq[:, c, :]))
                    nc.vector.tensor_tensor(acc[:, c, :], acc[:, c, :], sq[:, c, :], ALU.mult
                                            ).then_inc(norm_ready, 1)

            @block.scalar
            def _(act):
                n = 0
                for t in range(NT):
                    for c in range(2):
                        act.wait_ge(half_ready, n + 1)
                        nc.scalar.activation(half[:, t, c].rearrange("p s n -> p (s n)"), ps[:, 4 + n % 2, 0:2 * P],
                                             ACT.Copy).then_inc(half_read, 1)
                        n += 1
                n = 0
                for first, rows, tiles, tab in segs:
                    for c in range(2):
                        act.wait_ge(seq_ready, n + 1)
                        nc.scalar.activation(mixT[:, 4 + c, first:first + rows], ps[:, 6 + n % 2, 0:rows],
                                             ACT.Copy).then_inc(half_read, 1)
                        n += 1
                for c in range(2):
                    act.wait_ge(cent_ready, 2 * c + 2)
                    nc.scalar.activation(sq[:, c, :], acc[:, c, :], ACT.Square).then_inc(sq_ready, 1)
                    act.wait_ge(var_ready, c + 1)
                    nc.scalar.activation(sq[:, c, 0:512], ps[:, 2, :], ACT.Sqrt, bias=kit.eps[:, 0:1])
                    nc.scalar.activation(sq[:, c, 512:T], ps[:, 3, 0:T - 512], ACT.Sqrt, bias=kit.eps[:, 0:1]
                                         ).then_inc(root_ready, 1)
                    act.wait_ge(norm_ready, c + 1)
                    nc.scalar.activation(mixT[:, 6 + c, :], acc[:, c, :], ACT.Silu,
                                         bias=kit.prm[:, PRM["gnb"] + c:PRM["gnb"] + c + 1],
                                         scale=kit.prm[:, PRM["gnw"] + c:PRM["gnw"] + c + 1])

            @block.tensor
            def _(pe):
                n = 0
                for t in range(NT):
                    for c in range(2):
                        if n >= 2:
                            pe.wait_ge(half_read, n - 1)
                        nc.tensor.matmul(ps[:, 4 + n % 2, 0:2 * P], fT[:, c, t * P:(t + 1) * P],
                                         kit.c2("C64"), start=True, stop=True).then_inc(half_ready, 1)
                        n += 1
                pe.wait_ge(dft_in, 64)
                pe.wait_ge(half_read, n)
                m = 0
                for first, rows, tiles, tab in segs:
                    for c in range(2):
                        if m >= 2:
                            pe.wait_ge(half_read, n + m - 1)
                        for i in range(tiles):
                            for s in range(2):
                                last = nc.tensor.matmul(ps[:, 6 + m % 2, 0:rows], half[:, first // P + i, c, s, :],
                                                        tables[tab][:, i, s, :], start=(i, s) == (0, 0),
                                                        stop=(i, s) == (tiles - 1, 1))
                        last.then_inc(seq_ready, 1)
                        m += 1
                for c in range(2):
                    pe.wait_ge(convolved[c], 2)
                    if c:
                        pe.wait_ge(cent_ready, 2 * c)
                    nc.tensor.matmul(ps[:, 0, :], kit.c("gmean"), acc[:, c, 0:512], start=True, stop=True)
                    nc.tensor.matmul(ps[:, 1, 0:T - 512], kit.c("gmean"), acc[:, c, 512:T], start=True, stop=True
                                     ).then_inc(mean_ready, 1)
                    pe.wait_ge(sq_ready, c + 1)
                    nc.tensor.matmul(ps[:, 2, :], kit.c("gmean"), sq[:, c, 0:512], start=True, stop=True)
                    nc.tensor.matmul(ps[:, 3, 0:T - 512], kit.c("gmean"), sq[:, c, 512:T], start=True, stop=True
                                     ).then_inc(var_ready, 1)


def gdn_tiles(nc, kit, L, qkvT, gate, kt, u, wT, qkd, dec):
    G = 2 * H
    NL = len(LEVELS) - 1
    with ExitStack() as mem, phase(
            nc, kit, "rows_turned", "rows_ready", "gram_ready", "gram_used", "sums_ready", "dec_ready",
            "gmask_ready", "diff_ready", "exp_ready", "a_ready", "qk_ready", "block_ready", "inv1_ready",
            "inv1_turned", "invT1_ready", "w_ready", "w_copied", "upd_ready", "upd_done", "rhs_ready",
            "uw_ready", "uw_copied", "dve_step", "pool_step") as (
            rows_turned, rows_ready, gram_ready, gram_used, sums_ready, dec_ready,
            gmask_ready, diff_ready, exp_ready, a_ready, qk_ready, block_ready, inv1_ready,
            inv1_turned, invT1_ready, w_ready, w_copied, upd_ready, upd_done, rhs_ready,
            uw_ready, uw_copied, dve_step, pool_step):
        sb = lambda n, s: mem.enter_context(nc.sbuf_tensor(f"gd{n}_{L}", s, FP32))
        ra = sb("ra", [P, 2, H, P])
        rb = sb("rb", [P, 2, H, P])
        inv = sb("inv", [P, 2, H, P])
        invT = sb("invT", [P, 2, H, P])
        blk = sb("blk", [P, 2, H, P])
        vt = sb("vt", [P, H, P])
        bg = sb("bg", [P, 2, H])
        ps = kit.ps
        ident = kit.c("ident")
        wide = lambda a: a[:, :, None].to_broadcast([P, H, P])
        heads = lambda a: a[:, None, :].to_broadcast([P, H, P])
        bank = lambda b: ps[:, b, :].rearrange("p (h n) -> p h n", h=H)
        last_level = lambda t, d: 2 * NL * t + 2 * (NL - 1) + d + 1

        with nc.Block() as block:
            @block.tensor
            def _(pe):
                for t in range(NT):
                    tok = slice(t * P, (t + 1) * P)
                    if t:
                        pe.wait_ge(rows_ready, t)
                    for h in range(H):
                        nc.tensor.transpose(bank(0)[:, h, :], qkvT[:, H + h, tok], ident)
                    for h in range(H):
                        last = nc.tensor.transpose(bank(1)[:, h, :], qkvT[:, 2 * H + h, tok], ident)
                    last.then_inc(rows_turned, 1)
                    if t:
                        pe.wait_ge(gram_used, 2 * t)
                    for h in range(H):
                        nc.tensor.matmul(bank(2)[:, h, :], qkvT[:, H + h, tok], qkvT[:, H + h, tok],
                                         start=True, stop=True)
                    for h in range(H):
                        last = nc.tensor.matmul(bank(3)[:, h, :], qkvT[:, H + h, tok], qkvT[:, h, tok],
                                                start=True, stop=True)
                    last.then_inc(gram_ready, 1)
                    if t:
                        pe.wait_ge(uw_copied, 2 * t)
                    for d in range(2):
                        for kind, m in enumerate((f"L{d}", f"M{d}", "CH0", "CH1")):
                            col = (4 * d + kind) * H
                            last = nc.tensor.matmul(ps[:, 4, col:col + H], kit.c(m), gate[:, t, d * H:(d + 1) * H],
                                                    start=True, stop=True)
                    last.then_inc(sums_ready, 1)
                    pe.wait_ge(dec_ready, t + 1)
                    for d in range(2):
                        pe.wait_ge(gmask_ready, 2 * t + d + 1)
                        nc.tensor.matmul(ps[:, 4 + 2 * d, :], kit.c(f"L{d}"), ra[:, d].rearrange("p h n -> p (h n)"),
                                         start=True, stop=True)
                        nc.tensor.matmul(ps[:, 5 + 2 * d, :], kit.c(f"M{d}"), rb[:, d].rearrange("p h n -> p (h n)"),
                                         start=True, stop=True).then_inc(diff_ready, 1)
                    for d in range(2):
                        pe.wait_ge(inv1_ready, 2 * t + d + 1)
                        for h in range(H):
                            last = nc.tensor.transpose(bank(5 + 2 * d)[:, h, :], inv[:, d, h, :], ident)
                        last.then_inc(inv1_turned, 1)
                    for n in range(NL):
                        for d in range(2):
                            m = 2 * NL * t + 2 * n + d
                            pe.wait_ge(block_ready, 2 * (NL + 1) * t + 2 * (n + 1) + d + 1)
                            if n == 0:
                                pe.wait_ge(invT1_ready, 2 * t + d + 1)
                            else:
                                pe.wait_ge(upd_done, m - 1)
                            for h in range(H):
                                last = nc.tensor.matmul(bank(4 + 2 * d)[:, h, :], blk[:, d, h, :], invT[:, d, h, :],
                                                        start=True, stop=True)
                            last.then_inc(w_ready, 1)
                        for d in range(2):
                            pe.wait_ge(w_copied, 2 * NL * t + 2 * n + d + 1)
                            for h in range(H):
                                last = nc.tensor.matmul(bank(5 + 2 * d)[:, h, :], inv[:, d, h, :], rb[:, d, h, :],
                                                        start=True, stop=True)
                            if n < NL - 1:
                                for h in range(H):
                                    last = nc.tensor.matmul(bank(4 + 2 * d)[:, h, :], rb[:, d, h, :], inv[:, d, h, :],
                                                            start=True, stop=True)
                            last.then_inc(upd_ready, 1)
                    for d in range(2):
                        pe.wait_ge(upd_done, last_level(t, d))
                        pe.wait_ge(rhs_ready, 2 * t + d + 1)
                        for h in range(H):
                            nc.tensor.matmul(bank(5 + 2 * d)[:, h, :], invT[:, d, h, :], u[:, d, t, h, :],
                                             start=True, stop=True)
                        for h in range(H):
                            last = nc.tensor.matmul(bank(4 + 2 * d)[:, h, :], wT[:, d, t, h, :], invT[:, d, h, :],
                                                    start=True, stop=True)
                        last.then_inc(uw_ready, 1)

            @block.scalar
            def _(act):
                for t in range(NT):
                    act.wait_ge(rows_turned, t + 1)
                    nc.scalar.activation(kt[:, t], bank(0), ACT.Copy)
                    if t:
                        act.wait_ge(rhs_ready, 2 * t)
                    nc.scalar.activation(vt[:], bank(1), ACT.Copy).then_inc(rows_ready, 1)
                    act.wait_ge(sums_ready, t + 1)
                    nc.scalar.activation(dec[:, t].rearrange("p d k h -> p (d k h)"), ps[:, 4, 0:8 * H], ACT.Exp
                                         ).then_inc(dec_ready, 1)
                    for d in range(2):
                        act.wait_ge(diff_ready, 2 * t + d + 1)
                        nc.scalar.activation(ra[:, d], bank(4 + 2 * d), ACT.Exp)
                        nc.scalar.activation(rb[:, d], bank(5 + 2 * d), ACT.Exp).then_inc(exp_ready, 1)
                    for d in range(2):
                        act.wait_ge(inv1_turned, 2 * t + d + 1)
                        nc.scalar.activation(invT[:, d], bank(5 + 2 * d), ACT.Copy).then_inc(invT1_ready, 1)
                    for n in range(NL):
                        for d in range(2):
                            m = 2 * NL * t + 2 * n + d
                            if n == 0:
                                act.wait_ge(qk_ready, 2 * t + d + 1)
                            act.wait_ge(w_ready, m + 1)
                            nc.scalar.activation(rb[:, d], bank(4 + 2 * d), ACT.Copy).then_inc(w_copied, 1)
                    for d in range(2):
                        act.wait_ge(uw_ready, 2 * t + d + 1)
                        nc.scalar.activation(u[:, d, t], bank(5 + 2 * d), ACT.Copy)
                        nc.scalar.activation(wT[:, d, t], bank(4 + 2 * d), ACT.Copy).then_inc(uw_copied, 1)

            @block.vector
            def _(dve):
                link = linker(dve, dve_step)
                for t in range(NT):
                    dve.wait_ge(gram_ready, t + 1)
                    for d in range(2):
                        beta = gate[:, t, G + d * H:G + (d + 1) * H]
                        dve.wait_ge(exp_ready, 2 * t + d + 1)
                        link(nc.vector.tensor_tensor(ra[:, d], ra[:, d], bank(2), ALU.mult))
                        nc.vector.tensor_tensor(ra[:, d], ra[:, d], wide(beta), ALU.mult).then_inc(a_ready, 1)
                        nc.vector.tensor_tensor(qkd[:, d, t], rb[:, d], bank(3), ALU.mult).then_inc(gram_used, 1)
                        dve.wait_ge(gram_used, 2 * t + d + 1)
                        nc.vector.tensor_tensor(qkd[:, d, t], qkd[:, d, t], heads(kit.c(f"L{d}")), ALU.mult
                                                ).then_inc(qk_ready, 1)
                    for d in range(2):
                        dve.wait_ge(block_ready, 2 * (NL + 1) * t + d + 1)
                        nc.vector.tensor_tensor(inv[:, d], heads(ident), blk[:, d], ALU.subtract
                                                ).then_inc(inv1_ready, 1)
                    for n in range(NL):
                        for d in range(2):
                            m = 2 * NL * t + 2 * n + d
                            dve.wait_ge(upd_ready, m + 1)
                            op = nc.vector.tensor_tensor(invT[:, d], invT[:, d], bank(5 + 2 * d), ALU.subtract)
                            if n < NL - 1:
                                op = nc.vector.tensor_tensor(inv[:, d], inv[:, d], bank(4 + 2 * d), ALU.subtract)
                            op.then_inc(upd_done, 1)

            @block.gpsimd
            def _(pool):
                link = linker(pool, pool_step)
                for t in range(NT):
                    for d in range(2):
                        if t:
                            pool.wait_ge(upd_ready, last_level(t - 1, d))
                        g = gate[:, t, d * H:(d + 1) * H]
                        link(nc.gpsimd.tensor_tensor(ra[:, d], heads(kit.c(f"M{d}")), wide(g), ALU.mult))
                        nc.gpsimd.tensor_tensor(rb[:, d], heads(kit.c(f"L{d}")), wide(g), ALU.mult
                                                ).then_inc(gmask_ready, 1)
                    pool.wait_ge(rows_ready, t + 1)
                    pool.wait_ge(dec_ready, t + 1)
                    for d in range(2):
                        beta = gate[:, t, G + d * H:G + (d + 1) * H]
                        link(nc.gpsimd.tensor_tensor(u[:, d, t], vt[:], wide(beta), ALU.mult))
                        link(nc.gpsimd.tensor_tensor(bg[:, d], dec[:, t, d, 0, :], beta, ALU.mult))
                        nc.gpsimd.tensor_tensor(wT[:, d, t], kt[:, t], wide(bg[:, d]), ALU.mult
                                                ).then_inc(rhs_ready, 1)
                    for n in range(NL + 1):
                        for d in range(2):
                            if n == 0:
                                pool.wait_ge(a_ready, 2 * t + d + 1)
                                if t:
                                    pool.wait_ge(w_ready, last_level(t - 1, d))
                            elif n == 1:
                                pool.wait_ge(inv1_ready, 2 * t + d + 1)
                            else:
                                pool.wait_ge(w_ready, 2 * NL * t + 2 * (n - 2) + d + 1)
                            nc.gpsimd.tensor_tensor(blk[:, d], ra[:, d], heads(kit.c(f"B{d}_{n}")), ALU.mult
                                                    ).then_inc(block_ready, 1)


def gdn_scan(nc, kit, L, qkvT, kt, u, wT, qkd, dec, o):
    NCH = T // CHUNK
    CC = CTX // CHUNK
    with ExitStack() as mem, phase(nc, kit, "zeroed", "vo_ready", "vnew_ready", "os_ready", "state_ready",
                                   "tail_ready", "decayed", "o_ready", "dve_step") as (
            zeroed, vo_ready, vnew_ready, os_ready, state_ready, tail_ready, decayed, o_ready, dve_step):
        sb = lambda n, s: mem.enter_context(nc.sbuf_tensor(f"sc{n}_{L}", s, FP32))
        S = sb("S", [P, 2, H, P])
        Sd = sb("Sd", [P, 2, H, P])
        vn = sb("vn", [P, 2, H, P])
        tail = sb("tail", [P, 2, H, P])
        part = sb("part", [P, 2, H, P])
        ps = kit.ps
        bank = lambda b: ps[:, b, :].rearrange("p (h n) -> p h n", h=H)

        def place(s, d):
            c = s if d == 0 else (CC - 1 - s if s < CC else NCH - 1 + CC - s)
            return c // 2, c % 2, slice(CHUNK * (c % 2), CHUNK * (c % 2 + 1))

        with nc.Block() as block:
            @block.tensor
            def _(pe):
                pe.wait_ge(zeroed, 2)
                for s in range(NCH):
                    for d in range(2):
                        t, half, R = place(s, d)
                        tok = slice(t * P + R.start, t * P + R.stop)
                        if s:
                            pe.wait_ge(state_ready, 2 * (s - 1) + d + 1)
                            pe.wait_ge(o_ready, 2 * (s - 1) + d + 1)
                        for h in range(H):
                            nc.tensor.matmul(bank(4 * d)[R, h, :], wT[:, d, t, h, R], S[:, d, h, :],
                                             start=True, stop=True)
                        for h in range(H):
                            last = nc.tensor.matmul(bank(4 * d + 1)[R, h, :], qkvT[:, h, tok], S[:, d, h, :],
                                                    start=True, stop=True)
                        last.then_inc(vo_ready, 1)
                    for d in range(2):
                        t, half, R = place(s, d)
                        pe.wait_ge(vnew_ready, 2 * s + d + 1)
                        pe.wait_ge(tail_ready, 2 * s + d + 1)
                        for h in range(H):
                            nc.tensor.matmul(bank(4 * d + 3)[:, h, :], tail[R, d, h, :], vn[R, d, h, :],
                                             start=True, stop=True)
                        for h in range(H):
                            last = nc.tensor.matmul(bank(4 * d + 2)[R, h, :], qkd[R, d, t, h, R], vn[R, d, h, :],
                                                    start=True, stop=True)
                        last.then_inc(os_ready, 1)

            @block.vector
            def _(dve):
                link = linker(dve, dve_step)
                nc.vector.memset(S[:], 0.0).then_inc(zeroed, 1)
                nc.vector.memset(o[:], 0.0).then_inc(zeroed, 1)
                for s in range(NCH):
                    for d in range(2):
                        t, half, R = place(s, d)
                        dve.wait_ge(vo_ready, 2 * s + d + 1)
                        nc.vector.tensor_tensor(vn[R, d], u[R, d, t], bank(4 * d)[R], ALU.subtract
                                                ).then_inc(vnew_ready, 1)
                        link(nc.vector.tensor_tensor(part[R, d], bank(4 * d + 1)[R],
                                                     dec[R, t, d, 0, :][:, :, None].to_broadcast([CHUNK, H, P]),
                                                     ALU.mult))
                        link(nc.vector.tensor_tensor(o[R, t], o[R, t], part[R, d], ALU.add))
                    for d in range(2):
                        t, half, R = place(s, d)
                        dve.wait_ge(os_ready, 2 * s + d + 1)
                        dve.wait_ge(decayed, 2 * s + d + 1)
                        nc.vector.tensor_tensor(S[:, d], Sd[:, d], bank(4 * d + 3), ALU.add
                                                ).then_inc(state_ready, 1)
                        nc.vector.tensor_tensor(o[R, t], o[R, t], bank(4 * d + 2)[R], ALU.add
                                                ).then_inc(o_ready, 1)

            @block.gpsimd
            def _(pool):
                pool.wait_ge(zeroed, 2)
                for s in range(NCH):
                    for d in range(2):
                        t, half, R = place(s, d)
                        if s:
                            pool.wait_ge(os_ready, 2 * (s - 1) + d + 1)
                        nc.gpsimd.tensor_tensor(tail[R, d], kt[R, t],
                                                dec[R, t, d, 1, :][:, :, None].to_broadcast([CHUNK, H, P]),
                                                ALU.mult).then_inc(tail_ready, 1)
                        pool.wait_ge(tail_ready, 2 * s + d + 1)
                        if s:
                            pool.wait_ge(state_ready, 2 * (s - 1) + d + 1)
                        nc.gpsimd.tensor_tensor(Sd[:, d], S[:, d],
                                                dec[:, t, d, 2 + half, :][:, :, None].to_broadcast([P, H, P]),
                                                ALU.mult).then_inc(decayed, 1)
                        pool.wait_ge(decayed, 2 * s + d + 1)


def gdn_out(nc, kit, L, o, zs, mixT):
    with ExitStack() as mem, phase(nc, kit, "gain_in", "ms_ready", "root_ready", "y_ready", "turned", "copied",
                                   "dve_step") as (
            gain_in, ms_ready, root_ready, y_ready, turned, copied, dve_step):
        sb = lambda n, s: mem.enter_context(nc.sbuf_tensor(f"go{n}_{L}", s, FP32))
        gain = sb("gain", [P, P])
        sq = sb("sq", [P, NT * H, P])
        ss = sb("ss", [P, 2, NT * H])
        ps = kit.ps
        y = o[:].rearrange("p t h n -> p (t h) n")

        with nc.Block() as block:
            @block.sync
            def _(sp):
                sp.dma_start(gain[:], kit.gdn_norm[L:L + 1, :].broadcast_to([P, P])).then_inc(gain_in, 16)

            @block.vector
            def _(dve):
                link = linker(dve, dve_step)
                link(nc.vector.tensor_tensor(sq[:], y, y, ALU.mult))
                link(nc.vector.tensor_reduce(ss[:, 0, :], sq[:], AXX, ALU.add))
                nc.vector.tensor_scalar(ss[:, 1, :], ss[:, 0, :], 1.0 / P, EPS, ALU.mult, ALU.add
                                        ).then_inc(ms_ready, 1)
                dve.wait_ge(gain_in, 16)
                link(nc.vector.tensor_tensor(y, y, gain[:, None, :].to_broadcast([P, NT * H, P]), ALU.mult))
                link(nc.vector.tensor_tensor(y, y, zs[:].rearrange("p t (h n) -> p (t h) n", h=H), ALU.mult))
                dve.wait_ge(root_ready, 1)
                link(nc.vector.reciprocal(ss[:, 1, :], ss[:, 0, :]))
                nc.vector.tensor_tensor(y, y, ss[:, 1, :][:, :, None].to_broadcast([P, NT * H, P]), ALU.mult
                                        ).then_inc(y_ready, 1)

            @block.scalar
            def _(act):
                act.wait_ge(ms_ready, 1)
                nc.scalar.activation(ss[:, 0, :], ss[:, 1, :], ACT.Sqrt).then_inc(root_ready, 1)
                for t in range(NT):
                    act.wait_ge(turned, t + 1)
                    nc.scalar.activation(mixT[:, 0:H, t * P:(t + 1) * P],
                                         ps[:, t % 4, :].rearrange("p (h n) -> p h n", h=H), ACT.Copy
                                         ).then_inc(copied, 1)

            @block.tensor
            def _(pe):
                pe.wait_ge(y_ready, 1)
                for t in range(NT):
                    if t >= 4:
                        pe.wait_ge(copied, t - 3)
                    for h in range(H):
                        last = nc.tensor.transpose(ps[:, t % 4, h * P:(h + 1) * P], o[:, t, h, :], kit.c("ident"))
                    last.then_inc(turned, 1)


def mix_out(nc, kit, L, tiles, mixT):
    with ExitStack() as mem, phase(nc, kit, "w_arrived", "gates_in", "x0", "x1", "prod_ready", "gated", "sum_ready",
                                   "stored0", "stored1") as (
            w_arrived, gates_in, x0, x1, prod_ready, gated, sum_ready, stored0, stored1):
        x_in, stored = [x0, x1], [stored0, stored1]
        sb = lambda n, s: mem.enter_context(nc.sbuf_tensor(f"mo{n}_{L}", s, FP32))
        xb = sb("x", [P, 2, 2, 512])
        yb = sb("y", [P, 2, 2, 512])
        ps = kit.ps

        w = sb("w", [P, KD, D])
        gates = sb("gates", [P, 2, D])

        def store(sp, i):
            t = tiles[i]
            sp.wait_ge(sum_ready, 2 * (i + 1))
            sp.dma_start(kit.x_d[t * P:(t + 1) * P, :], xb[:, i % 2].rearrange("p a n -> p (a n)")
                         ).then_inc(stored[i % 2], 16)

        with nc.Block() as block:
            @block.sync
            def _(sp):
                sp.dma_start(w[:], kit.w_out[L].rearrange("(k p) n -> p k n", p=P)).then_inc(w_arrived, 16)
                for g in range(2):
                    sp.dma_start(gates[:, g, :], mod_row(kit, g, 2)).then_inc(gates_in, 16)
                for i, t in enumerate(tiles):
                    b = i % 2
                    rows = kit.x_d[t * P:(t + 1) * P, :]
                    if i >= 2:
                        sp.wait_ge(stored[b], 16 * (i // 2))
                    sp.dma_start(xb[:, b].rearrange("p a n -> p (a n)"), rows).then_inc(x_in[b], 16)
                    if i >= 1:
                        store(sp, i - 1)
                store(sp, len(tiles) - 1)
                for b in range(2):
                    sp.wait_ge(stored[b], 16 * ((len(tiles) + 1 - b) // 2))

            @block.tensor
            def _(pe):
                pe.wait_ge(w_arrived, 16)
                for i, t in enumerate(tiles):
                    for half in range(2):
                        q = 2 * i + half
                        if q >= 4:
                            pe.wait_ge(gated, q - 3)
                        for k in range(KD):
                            last = nc.tensor.matmul(ps[:, q % 4, :], mixT[:, k, t * P:(t + 1) * P],
                                                    w[:, k, half * 512:(half + 1) * 512], start=k == 0,
                                                    stop=k == KD - 1)
                        last.then_inc(prod_ready, 1)

            @block.vector
            def _(dve):
                dve.wait_ge(gates_in, 32)
                for i, t in enumerate(tiles):
                    s = int(t >= NC)
                    dve.wait_ge(x_in[i % 2], 16 * (i // 2 + 1))
                    for half in range(2):
                        q = 2 * i + half
                        dve.wait_ge(prod_ready, q + 1)
                        nc.vector.tensor_tensor(yb[:, i % 2, half, :], ps[:, q % 4, :],
                                                gates[:, s, half * 512:(half + 1) * 512], ALU.mult
                                                ).then_inc(gated, 1)
                        dve.wait_ge(gated, q + 1)
                        nc.vector.tensor_tensor(xb[:, i % 2, half, :], xb[:, i % 2, half, :],
                                                yb[:, i % 2, half, :], ALU.add).then_inc(sum_ready, 1)


def peer_tables(nc, kit, L, tiles, wq, keysT):
    with ExitStack() as mem, phase(nc, kit, "wq_in", "keys_in", "rows_in", "turned", "copied", "scale_ready",
                                   "stored") as (wq_in, keys_in, rows_in, turned, copied, scale_ready, stored):
        sb = lambda n, s: mem.enter_context(nc.sbuf_tensor(f"pt{n}_{L}", s, FP32))
        keys = sb("keys", [P, HP, P])
        gain = sb("gain", [2, D])
        sc = sb("sc", [2, D])
        ps = kit.ps

        with nc.Block() as block:
            @block.sync
            def _(sp):
                sp.dma_start(sc[:], kit.mod_d[:, 4 * D:5 * D]).then_inc(rows_in, 16)
                sp.dma_start(gain[:], kit.norm2[L:L + 1, :].broadcast_to([2, D])).then_inc(rows_in, 16)
                sp.dma_start(keys[:], kit.peer_keys[L].rearrange("h s k d -> k (h s) d")).then_inc(keys_in, 16)
                sp.dma_start(wq[:], kit.peer_wq[L].rearrange("(k p) n -> p k n", p=P)).then_inc(wq_in, 16)
                for t in tiles:
                    s = int(t >= NC)
                    sp.dma_start(kit.rows_d[t, 1:2, :], kit.mod_d[s:s + 1, 3 * D:4 * D]).then_inc(stored, 16)
                    sp.dma_start(kit.rows_d[t, 2:3, :], kit.mod_d[s:s + 1, 5 * D:6 * D]).then_inc(stored, 16)
                sp.wait_ge(scale_ready, 1)
                for t in tiles:
                    s = int(t >= NC)
                    sp.dma_start(kit.rows_d[t, 0:1, :], sc[s:s + 1, :]).then_inc(stored, 16)
                sp.wait_ge(stored, 48 * len(tiles))
                sp.wait_ge(wq_in, 16)

            @block.vector
            def _(dve):
                dve.wait_ge(rows_in, 32)
                nc.vector.scalar_tensor_tensor(out=sc[:], in0=sc[:], scalar=1.0, in1=gain[:], op0=ALU.add,
                                               op1=ALU.mult).then_inc(scale_ready, 1)

            @block.tensor
            def _(pe):
                pe.wait_ge(keys_in, 16)
                for q in range(HP // 4):
                    for i in range(4):
                        last = nc.tensor.transpose(ps[:, q, i * P:(i + 1) * P], keys[:, 4 * q + i, :],
                                                   kit.c("ident"))
                    last.then_inc(turned, 1)

            @block.scalar
            def _(act):
                for q in range(HP // 4):
                    act.wait_ge(turned, q + 1)
                    nc.scalar.activation(keysT[:, 4 * q:4 * q + 4, :].rearrange("p h n -> p (h n)"), ps[:, q, :],
                                         ACT.Copy).then_inc(copied, 1)


def peer_tile(nc, kit, L, m, cur, nxt):
    GROUP = 16
    NG = SLOTS // GROUP
    RING = kit.ring
    DG = 4
    QC = 4
    NQ = HP // QC
    u_tab = kit.peer_u.rearrange("l e d -> (l e) d")
    v_tab = kit.peer_v.rearrange("l e d -> (l e) d")
    names = (["u%d" % i for i in range(RING)] + ["v%d" % i for i in range(RING)]
             + ["u_used", "gelu_ready", "coef_ready", "diag_ready", "v_used", "xg_in", "y_gated", "x_ready",
                "stored", "row_in", "ss_ready", "ms_ready", "root_ready", "h_ready", "h_turned", "hT_ready",
                "q_ready", "q_copied", "s_ready", "s_copied", "picked", "top_ready", "soft_ready", "eid_ready",
                "shifted", "dve_step"])
    with phase(nc, kit, *names, gathers=2 * RING) as sems:
        u_in, v_in = sems[:RING], sems[RING:2 * RING]
        (u_used, gelu_ready, coef_ready, diag_ready, v_used, xg_in, y_gated, x_ready, stored, row_in, ss_ready,
         ms_ready, root_ready, h_ready, h_turned, hT_ready, q_ready, q_copied, s_ready, s_copied, picked,
         top_ready, soft_ready, eid_ready, shifted, dve_step) = sems[2 * RING:]
        ps = kit.ps
        ident = kit.c("ident")
        row = lambda ap, t: ap[bass.ds(t, 1), :, :].rearrange("a p n -> p (a n)")
        x_t = kit.x_d.rearrange("(t p) n -> t p n", p=P)

        with nc.Block() as block:
            @block.sync
            def _(sp):
                if nxt is not None:
                    sp.dma_start(m.xn[:], row(x_t, nxt)).then_inc(row_in, 16)
                    for i in range(2):
                        sp.dma_start(m.mod[:, i, :], kit.rows_d[bass.ds(nxt, 1), i, :].broadcast_to([P, D])
                                     ).then_inc(row_in, 16)
                if cur is not None:
                    sp.dma_start(m.xc[:], row(x_t, cur)).then_inc(xg_in, 16)
                    sp.dma_start(m.gate_c[:], kit.rows_d[bass.ds(cur, 1), 2, :].broadcast_to([P, D])
                                 ).then_inc(xg_in, 16)
                    sp.wait_ge(x_ready, 1)
                    sp.dma_start(row(x_t, cur), m.xc[:]).then_inc(stored, 16)
                    sp.wait_ge(stored, 16)

            @block.gpsimd
            def _(pool):
                if cur is None:
                    return
                for g in range(NG + 1):
                    for i in range(GROUP):
                        if g < NG:
                            k = g * GROUP + i
                            if k >= RING:
                                pool.wait_ge(u_used, k - RING + 1)
                            nc.gpsimd.indirect_dma_start(
                                m.ub[:, k % RING, :], None, u_tab,
                                bass.IndirectOffsetOnAxis(m.eid[:, k:k + 1], 0)).then_inc(u_in[k % RING], 16)
                        if g >= 1:
                            k = (g - 1) * GROUP + i
                            if k >= RING:
                                pool.wait_ge(v_used, k - RING + 1)
                            nc.gpsimd.indirect_dma_start(
                                m.vb[:, k % RING, :], None, v_tab,
                                bass.IndirectOffsetOnAxis(m.eid[:, k:k + 1], 0)).then_inc(v_in[k % RING], 16)
                for s in u_in + v_in:
                    pool.wait_ge(s, 16 * (SLOTS // RING))

            @block.vector
            def _(dve):
                link = linker(dve, dve_step)

                def dots(g):
                    for k in range(g * GROUP, (g + 1) * GROUP):
                        dve.wait_ge(u_in[k % RING], 16 * (k // RING + 1))
                        if k:
                            dve.wait_ge(u_used, k)
                        nc.vector.tensor_tensor_reduce(out=m.dot[:], in0=m.ub[:, k % RING, :], in1=m.hc[:],
                                                       scale=1.0, scalar=0.0, op0=ALU.mult, op1=ALU.add,
                                                       accum_out=m.act[:, k:k + 1]).then_inc(u_used, 1)
                    G = slice(g * GROUP, (g + 1) * GROUP)
                    dve.wait_ge(gelu_ready, g + 1)
                    nc.vector.tensor_tensor(m.coef[:, G], m.coef[:, G], m.gw[:, G], ALU.mult
                                            ).then_inc(coef_ready, 1)

                def norm():
                    dve.wait_ge(ss_ready, 1)
                    nc.vector.tensor_scalar(m.ss[:, 1:2], m.ss[:, 0:1], 1.0 / D, EPS, ALU.mult, ALU.add
                                            ).then_inc(ms_ready, 1)
                    dve.wait_ge(root_ready, 1)
                    link(nc.vector.reciprocal(m.ss[:, 3:4], m.ss[:, 2:3]))
                    dve.wait_ge(row_in, 48)
                    link(nc.vector.scalar_tensor_tensor(out=m.hn[:], in0=m.xn[:], scalar=m.ss[:, 3:4],
                                                        in1=m.mod[:, 0, :], op0=ALU.mult, op1=ALU.mult))
                    nc.vector.tensor_tensor(m.hn[:], m.hn[:], m.mod[:, 1, :], ALU.add).then_inc(h_ready, 1)

                def top16(val, idx, src, rest):
                    link(nc.vector.max(val[:, 0:8], src))
                    link(nc.vector.max_index(idx[:, 0:8], val[:, 0:8], src))
                    link(nc.vector.match_replace(rest, val[:, 0:8], src, NEG))
                    link(nc.vector.max(val[:, 8:16], rest))
                    link(nc.vector.max_index(idx[:, 8:16], val[:, 8:16], rest))

                def pick(j):
                    dve.wait_ge(s_copied, j + 1)
                    for i in range(QC):
                        q = QC * j + i
                        top16(m.sv[:, q, :], m.si[:, q, :], m.s[:, j % 2, i, :], m.rest[:, 0:NKEYS])
                    nc.vector.tensor_copy(m.sif[:, QC * j:QC * (j + 1), :], m.si[:, QC * j:QC * (j + 1), :]
                                          ).then_inc(picked, 1)
                    dve.wait_ge(picked, j + 1)

                def combine():
                    for h in range(PH):
                        a = m.sv[:, 2 * h, :][:, :, None].to_broadcast([P, TOPK, TOPK])
                        b = m.sv[:, 2 * h + 1, :][:, None, :].to_broadcast([P, TOPK, TOPK])
                        link(nc.vector.tensor_tensor(m.cand[:].rearrange("p (a b) -> p a b", a=TOPK), a, b, ALU.add))
                        top16(m.fv[:, h, :], m.fi[:, h, :], m.cand[:], m.rest[:])
                    nc.vector.tensor_tensor(m.gn[:], m.fv[:], m.fv[:, :, 0:1].to_broadcast([P, PH, TOPK]),
                                            ALU.subtract).then_inc(top_ready, 1)
                    dve.wait_ge(soft_ready, 1)
                    link(nc.vector.tensor_reduce(m.gsum[:, 0, :], m.gn[:], AXX, ALU.add))
                    link(nc.vector.reciprocal(m.gsum[:, 1, :], m.gsum[:, 0, :]))
                    link(nc.vector.tensor_tensor(m.gn[:], m.gn[:],
                                                 m.gsum[:, 1, :][:, :, None].to_broadcast([P, PH, TOPK]), ALU.mult))

                def number():
                    fi = m.fi[:].rearrange("p h k -> p (h k)")
                    for side, (op, by) in enumerate(((ALU.logical_shift_right, 4), (ALU.bitwise_and, 15))):
                        link(nc.vector.tensor_scalar(m.place[:], fi, by, None, op))
                        link(nc.vector.tensor_copy(m.placef[:], m.place[:]))
                        eq = m.eq[:].rearrange("p (a b) -> p a b", b=TOPK)
                        link(nc.vector.tensor_tensor(eq, m.placef[:, :, None].to_broadcast([P, SLOTS, TOPK]),
                                                     kit.iota[:, None, :].to_broadcast([P, SLOTS, TOPK]),
                                                     ALU.is_equal))
                        eq4 = m.eq[:].rearrange("p (h a b) -> p h a b", a=TOPK, b=TOPK)
                        key = m.sif[:].rearrange("p (h s) k -> p h s k", s=2)[:, :, side, :]
                        link(nc.vector.tensor_tensor(eq4, eq4, key[:, :, None, :].to_broadcast(
                            [P, PH, TOPK, TOPK]), ALU.mult))
                        link(nc.vector.tensor_reduce(m.num[:, side, :], eq, AXX, ALU.add))
                    link(nc.vector.tensor_scalar(m.num[:, 0, :], m.num[:, 0, :], float(NKEYS), float(L * NKEYS * NKEYS),
                                                 ALU.mult, ALU.add))
                    nc.vector.tensor_tensor(m.num[:, 0, :], m.num[:, 0, :], m.num[:, 1, :], ALU.add
                                            ).then_inc(eid_ready, 1)
                    dve.wait_ge(eid_ready, 1)

                def part(g):
                    if nxt is None:
                        return
                    if g == 0:
                        norm()
                    elif g <= NQ:
                        pick(g - 1)
                    elif g == NQ + 1:
                        combine()
                    elif g == NQ + 2:
                        number()

                for g in range(NG):
                    if cur is not None:
                        dots(g)
                    part(g)
                if cur is not None:
                    dve.wait_ge(v_used, SLOTS)
                    dve.wait_ge(xg_in, 32)
                    nc.vector.tensor_tensor(m.dot[:], m.gate_c[:], ps[:, 0:2, :].rearrange("p b n -> p (b n)"), ALU.mult
                                            ).then_inc(y_gated, 1)
                    dve.wait_ge(y_gated, 1)
                    nc.vector.tensor_tensor(m.xc[:], m.xc[:], m.dot[:], ALU.add).then_inc(x_ready, 1)
                if nxt is not None:
                    dve.wait_ge(h_turned, 1)
                    nc.vector.tensor_copy(m.hc[:], m.hn[:]).then_inc(shifted, 1)
                    nc.vector.tensor_copy(m.gw[:], m.gn[:].rearrange("p h k -> p (h k)")).then_inc(shifted, 1)
                    nc.vector.tensor_copy(m.eid[:], m.num[:, 0, :]).then_inc(shifted, 1)
                    dve.wait_ge(shifted, 3)

            @block.scalar
            def _(act):
                def diagonals(g):
                    act.wait_ge(coef_ready, g + 1)
                    for k in range(g * GROUP, (g + 1) * GROUP):
                        if k >= DG:
                            act.wait_ge(v_used, k - DG + 1)
                        nc.scalar.activation(m.diag[:, k % DG, :], ident, ACT.Copy, scale=m.coef[:, k:k + 1]
                                             ).then_inc(diag_ready, 1)

                def part(g):
                    if nxt is None:
                        return
                    if g == 0:
                        act.wait_ge(row_in, 48)
                        nc.scalar.activation(m.hn[:], m.xn[:], ACT.Square, accum_out=m.ss[:, 0:1]
                                             ).then_inc(ss_ready, 1)
                        act.wait_ge(ms_ready, 1)
                        nc.scalar.activation(m.ss[:, 2:3], m.ss[:, 1:2], ACT.Sqrt).then_inc(root_ready, 1)
                        act.wait_ge(h_turned, 1)
                        nc.scalar.activation(m.hT[:].rearrange("p k n -> p (k n)"),
                                             ps[:, 2:4, :].rearrange("p b n -> p (b n)"), ACT.Copy
                                             ).then_inc(hT_ready, 1)
                    elif g <= NQ:
                        j = g - 1
                        act.wait_ge(q_ready, j + 1)
                        nc.scalar.activation(m.q[:].rearrange("p a n -> p (a n)"), ps[:, 4, :], ACT.Copy
                                             ).then_inc(q_copied, 1)
                        act.wait_ge(s_ready, j + 1)
                        if j >= 2:
                            act.wait_ge(picked, j - 1)
                        nc.scalar.activation(m.s[:, j % 2].rearrange("p a n -> p (a n)"), ps[:, 5, :], ACT.Copy
                                             ).then_inc(s_copied, 1)
                    elif g == NQ + 1:
                        act.wait_ge(top_ready, 1)
                        nc.scalar.activation(m.gn[:], m.gn[:], ACT.Exp).then_inc(soft_ready, 1)

                for g in range(NG + 1):
                    if cur is not None:
                        if g >= 1:
                            diagonals(g - 1)
                        if g < NG:
                            act.wait_ge(u_used, (g + 1) * GROUP)
                            nc.scalar.activation(m.coef[:, g * GROUP:(g + 1) * GROUP],
                                                 m.act[:, g * GROUP:(g + 1) * GROUP], ACT.Gelu_apprx_tanh
                                                 ).then_inc(gelu_ready, 1)
                    part(g)

            @block.tensor
            def _(pe):
                def add_rows(g):
                    for k in range(g * GROUP, (g + 1) * GROUP):
                        pe.wait_ge(v_in[k % RING], 16 * (k // RING + 1))
                        pe.wait_ge(diag_ready, k + 1)
                        for half in range(2):
                            last = nc.tensor.matmul(ps[:, half, :], m.diag[:, k % DG, :],
                                                    m.vb[:, k % RING, half * 512:(half + 1) * 512],
                                                    start=k == 0, stop=k == SLOTS - 1)
                        last.then_inc(v_used, 1)

                def part(g):
                    if nxt is None:
                        return
                    if g == 0:
                        pe.wait_ge(h_ready, 1)
                        for k in range(KD):
                            last = nc.tensor.transpose(ps[:, 2 + k // 4, (k % 4) * P:(k % 4 + 1) * P],
                                                       m.hn[:, k * P:(k + 1) * P], ident)
                        last.then_inc(h_turned, 1)
                        pe.wait_ge(hT_ready, 1)
                    elif g <= NQ:
                        j = g - 1
                        for i in range(QC):
                            q = QC * j + i
                            for k in range(KD):
                                last = nc.tensor.matmul(ps[:, 4, i * P:(i + 1) * P], m.wq[:, k, q * P:(q + 1) * P],
                                                        m.hT[:, k, :], start=k == 0, stop=k == KD - 1)
                        last.then_inc(q_ready, 1)
                        pe.wait_ge(q_copied, j + 1)
                        if j:
                            pe.wait_ge(s_copied, j)
                        for i in range(QC):
                            last = nc.tensor.matmul(ps[:, 5, i * P:(i + 1) * P], m.q[:, i, :],
                                                    m.keysT[:, QC * j + i, :], start=True, stop=True)
                        last.then_inc(s_ready, 1)

                for g in range(NG + 1):
                    if cur is not None and g >= 1:
                        add_rows(g - 1)
                    part(g)


def peer(nc, kit, L, first):
    with ExitStack() as mem:
        sb = lambda n, s, t=FP32: mem.enter_context(nc.sbuf_tensor(f"pe{n}_{L}", s, t))
        m = Kit()
        m.wq = sb("wq", [P, KD, HP * P])
        m.keysT = sb("keysT", [P, HP, P])
        peer_tables(nc, kit, L, range(first, NT), m.wq, m.keysT)
        m.hc, m.xc, m.gate_c = sb("hc", [P, D]), sb("xc", [P, D]), sb("gc", [P, D])
        m.eid, m.gw = sb("eid", [P, SLOTS], U32), sb("gw", [P, SLOTS])
        m.ub, m.vb = sb("ub", [P, kit.ring, D]), sb("vb", [P, kit.ring, D])
        m.dot, m.act, m.coef = sb("dot", [P, D]), sb("act", [P, SLOTS]), sb("coef", [P, SLOTS])
        m.diag = sb("diag", [P, 4, P])
        m.xn, m.hn, m.mod = sb("xn", [P, D]), sb("hn", [P, D]), sb("mod", [P, 2, D])
        m.ss, m.hT = sb("ss", [P, 4]), sb("hT", [P, KD, P])
        m.q, m.s = sb("q", [P, 4, P]), sb("s", [P, 2, 4, P])
        m.sv, m.sif = sb("sv", [P, HP, TOPK]), sb("sif", [P, HP, TOPK])
        m.rest, m.cand = sb("rest", [P, TOPK * TOPK]), sb("cand", [P, TOPK * TOPK])
        m.fv, m.gn, m.gsum = sb("fv", [P, PH, TOPK]), sb("gn", [P, PH, TOPK]), sb("gsum", [P, 2, PH])
        m.placef, m.eq, m.num = sb("placef", [P, SLOTS]), sb("eq", [P, SLOTS * TOPK]), sb("num", [P, 2, SLOTS])
        m.si = sb("si", [P, HP, TOPK], U32)
        m.fi = sb("fi", [P, PH, TOPK], U32)
        m.place = sb("place", [P, SLOTS], U32)
        peer_tile(nc, kit, L, m, None, first)
        with nc.Fori(first, NT - 1) as t:
            peer_tile(nc, kit, L, m, t, t + 1)
        peer_tile(nc, kit, L, m, NT - 1, None)


def final_norm(nc, kit):
    N = NT - NC
    with ExitStack() as mem, phase(nc, kit, "gain_in", "x_in", "ss_ready", "ms_ready", "root_ready", "y_ready",
                                   "stored", "dve_step") as (
            gain_in, x_in, ss_ready, ms_ready, root_ready, y_ready, stored, dve_step):
        sb = lambda n, s: mem.enter_context(nc.sbuf_tensor(f"fn{n}", s, FP32))
        gain = sb("gain", [P, D])
        x = sb("x", [P, N, D])
        sq = sb("sq", [P, D])
        ss = sb("ss", [P, 2, N])

        with nc.Block() as block:
            @block.sync
            def _(sp):
                sp.dma_start(x[:], kit.x_d[CTX:T, :].rearrange("(t p) n -> p t n", p=P)).then_inc(x_in, 16)
                sp.dma_start(gain[:], kit.final_norm.rearrange("(a n) -> a n", a=1).broadcast_to([P, D])
                             ).then_inc(gain_in, 16)
                for t in range(N):
                    sp.wait_ge(y_ready, t + 1)
                    sp.dma_start(kit.out[0, t * P:(t + 1) * P, :], x[:, t, :]).then_inc(stored, 16)
                sp.wait_ge(stored, 16 * N)

            @block.scalar
            def _(act):
                act.wait_ge(x_in, 16)
                for t in range(N):
                    if t:
                        act.wait_ge(ss_ready, t)
                    nc.scalar.activation(sq[:], x[:, t, :], ACT.Square, accum_out=ss[:, 0, t:t + 1]
                                         ).then_inc(ss_ready, 1)
                act.wait_ge(ms_ready, 1)
                nc.scalar.activation(ss[:, 0, :], ss[:, 1, :], ACT.Sqrt).then_inc(root_ready, 1)

            @block.vector
            def _(dve):
                link = linker(dve, dve_step)
                dve.wait_ge(ss_ready, N)
                nc.vector.tensor_scalar(ss[:, 1, :], ss[:, 0, :], 1.0 / D, EPS, ALU.mult, ALU.add
                                        ).then_inc(ms_ready, 1)
                dve.wait_ge(gain_in, 16)
                dve.wait_ge(root_ready, 1)
                link(nc.vector.reciprocal(ss[:, 1, :], ss[:, 0, :]))
                for t in range(N):
                    nc.vector.scalar_tensor_tensor(out=x[:, t, :], in0=x[:, t, :], scalar=ss[:, 1, t:t + 1],
                                                   in1=gain[:], op0=ALU.mult, op1=ALU.mult).then_inc(y_ready, 1)


def backbone(nc, kit, layers=range(DEPTH)):
    kit.phases = 0
    kit.ring = 4
    with ExitStack() as mem:
        sb = lambda n, s, t=FP32: mem.enter_context(nc.sbuf_tensor(n, s, t))
        kit.ps = mem.enter_context(nc.psum_tensor("ps", [P, 8, 512], FP32))
        kit.cst = sb("cst", [P, len(CONSTS) * P + TOPK])
        kit.iota = kit.cst[:, len(CONSTS) * P:]
        kit.eps = sb("eps", [P, 2])
        kit.prm = sb("prm", [P, NPRM])
        kit.x_d = nc.dram_tensor("x_rows", [T, D], FP32, kind="Internal").ap()
        kit.mod_d = nc.dram_tensor("mod_rows", [2, 6 * D], FP32, kind="Internal").ap()
        kit.rows_d = nc.dram_tensor("peer_rows", [NT, 3, D], FP32, kind="Internal").ap()
        setup(nc, kit)
        for L in layers:
            last = L == DEPTH - 1
            first = NC if last else 0
            modulation(nc, kit, L)
            with ExitStack() as lay:
                sl = lambda n, s: lay.enter_context(nc.sbuf_tensor(f"{n}_{L}", s, FP32))
                hT = sl("hT", [P, KD, T])
                qkvT = sl("qkvT", [P, NQKV, T])
                zs = sl("zs", [P, NT, GW])
                ab = sl("ab", [P, NT, 4 * H])
                gate = sl("gate", [P, NT, 4 * H])
                norm_in(nc, kit, L, hT)
                with ExitStack() as cv:
                    sc = lambda n, s: cv.enter_context(nc.sbuf_tensor(f"{n}_{L}", s, FP32))
                    fT, aT, gT = sc("fT", [P, 2, T]), sc("aT", [P, 2, T]), sc("gT", [P, 2, T])
                    projection(nc, kit, L, hT, qkvT, zs, ab, fT, aT, gT)
                    conv_and_fnet(nc, kit, L, fT, aT, gT, hT)
                unit_and_gates(nc, kit, L, qkvT, ab, gate)
                o = qkvT[:, 2 * H:3 * H, :].rearrange("p a b -> p (a b)").rearrange("p (t h n) -> p t h n", t=NT, h=H)
                with ExitStack() as gd:
                    sg = lambda n, s: gd.enter_context(nc.sbuf_tensor(f"{n}_{L}", s, FP32))
                    kt = sg("kt", [P, NT, H, P])
                    u, wT, qkd = sg("u", [P, 2, NT, H, P]), sg("wT", [P, 2, NT, H, P]), sg("qkd", [P, 2, NT, H, P])
                    dec = sg("dec", [P, NT, 2, 4, H])
                    gdn_tiles(nc, kit, L, qkvT, gate, kt, u, wT, qkd, dec)
                    gdn_scan(nc, kit, L, qkvT, kt, u, wT, qkd, dec, o)
                gdn_out(nc, kit, L, o, zs, hT)
                mix_out(nc, kit, L, list(range(first, NT)), hT)
            peer(nc, kit, L, first)
        final_norm(nc, kit)


def constants():
    import numpy as np

    i, j = np.arange(P)[:, None], np.arange(P)[None, :]
    same = i // CHUNK == j // CHUNK
    c = {"ident": i == j, "L0": same & (i <= j), "L1": same & (i >= j), "M0": same & (i > j),
         "M1": same & (i < j), "CH0": (i < CHUNK) & (j >= 0), "CH1": (i >= CHUNK) & (j >= 0),
         "ones": np.ones((P, P)), "gmean": (i // 64 == j // 64) / 64.0}
    ang = 2 * np.pi * ((i % 64) * (j % 64) % 64) / 64
    c["C64"], c["S64"] = (i // 64 == j // 64) * np.cos(ang), (i // 64 == j // 64) * np.sin(ang)
    for n, b in enumerate(LEVELS):
        pair = (i // (2 * b) == j // (2 * b))
        c[f"B0_{n}"], c[f"B1_{n}"] = pair & (i // b > j // b), pair & (i // b < j // b)
    cst = np.concatenate([np.asarray(c[k], np.float32) for k in CONSTS]
                         + [np.broadcast_to(np.arange(TOPK, dtype=np.float32), (P, TOPK))], axis=1)

    def dft(n):
        k = np.arange(n)
        a = 2 * np.pi * (np.outer(k, k) % n) / n
        s = 1 / np.sqrt(n * 64.0)
        return np.stack([np.cos(a) * s, -np.sin(a) * s]).astype(np.float32)

    return {"consts": np.ascontiguousarray(cst), "dft_l": dft(SEQ), "dft_c": dft(CTX)}


_INS = ["x", "c", "ctx", "c_ctx", "w_mod", "b_mod", "norm1", "norm2", "w_in", "conv_qkv", "a_log", "dt_bias",
        "gdn_norm", "dw_w", "dw_b", "gn_w", "gn_b", "w_out", "peer_wq", "peer_keys", "peer_u", "peer_v",
        "final_norm"]


def build(nc, a, out):
    kit = Kit()
    kit.x, kit.cnd, kit.ctx, kit.c_ctx = a["x"], a["c"], a["ctx"], a["c_ctx"]
    kit.w_mod, kit.b_mod, kit.norm1, kit.norm2 = a["w_mod"], a["b_mod"], a["norm1"], a["norm2"]
    kit.w_in, kit.conv_qkv, kit.a_log, kit.dt_bias = a["w_in"], a["conv_qkv"], a["a_log"], a["dt_bias"]
    kit.gdn_norm, kit.dw_w, kit.dw_b = a["gdn_norm"], a["dw_w"], a["dw_b"]
    kit.gn_w, kit.gn_b, kit.w_out = a["gn_w"], a["gn_b"], a["w_out"]
    kit.peer_wq, kit.peer_keys, kit.peer_u, kit.peer_v = a["peer_wq"], a["peer_keys"], a["peer_u"], a["peer_v"]
    kit.final_norm, kit.consts, kit.dft_l, kit.dft_c = a["final_norm"], a["consts"], a["dft_l"], a["dft_c"]
    kit.out = out
    backbone(nc, kit)


def kernel(**inputs):
    import numpy as _np
    import concourse.bacc as _bacc
    from concourse.bass_utils import run_bass_kernel_spmd as _run

    nc = _bacc.Bacc("TRN2", target_bir_lowering=False, num_devices=1)
    arrays, args = {}, {}
    for name, a in [(n, inputs[n]) for n in _INS] + list(constants().items()):
        a = _np.ascontiguousarray(a)
        arrays[f"in_{name}_dram"] = a
        args[name] = nc.dram_tensor(f"in_{name}_dram", a.shape, mybir.dt.from_np(a.dtype), kind="ExternalInput").ap()
    out = nc.dram_tensor("out_0_dram", (1, SEQ, D), FP32, kind="ExternalOutput").ap()
    build(nc, args, out)
    r = _run(nc, [arrays], core_ids=[0])
    return r.results[0]["out_0_dram"]
```

```python
import concourse.bass as bass
from concourse import mybir
from contextlib import ExitStack, contextmanager

FP32 = mybir.dt.float32
U32 = mybir.dt.uint32
ALU = mybir.AluOpType
ACT = mybir.ActivationFunctionType
AXX = mybir.AxisListType.X

P = 128
D = 1024
KD = D // P
SEQ, CTX = 512, 256
T = SEQ + CTX
NT = T // P
NC = CTX // P
DEPTH = 2
GRID_W = 64
H = 4
GW = H * P
CHUNK = 64
IN_W = 4 * GW + 4 * H + 256 + 512
Z_OFF, A_OFF = 3 * GW, 4 * GW
F_OFF = A_OFF + 4 * H
C_OFF = F_OFF + 256
NQKV = 3 * GW // P
TAPS, CONV_K = 3, 31
HALO = CONV_K // 2
PH, NKEYS, TOPK = 8, 128, 16
HP = 2 * PH
SLOTS = PH * TOPK
EPS = 1e-6
LEVELS = [1, 2, 4, 8, 16, 32]
NEG = -3.0e38

CONSTS = (["ident", "L0", "L1", "M0", "M1", "CH0", "CH1", "ones", "gmean", "C64", "S64"]
          + [f"B{d}_{n}" for d in range(2) for n in range(len(LEVELS))])
PRM = {"conv": 0, "dw": TAPS * NQKV, "dwb": TAPS * NQKV + 2 * CONV_K}
PRM["gnw"] = PRM["dwb"] + 2
PRM["gnb"] = PRM["gnw"] + 2
NPRM = PRM["gnb"] + 2


class Kit:

    def c(self, name):
        at = CONSTS.index(name) * P
        return self.cst[:, at:at + P]

    def c2(self, name):
        at = CONSTS.index(name) * P
        return self.cst[:, at:at + 2 * P]


def runs(numbers):
    found = []
    for n in sorted(numbers):
        if found and found[-1].stop == n:
            found[-1] = range(found[-1].start, n + 1)
        else:
            found.append(range(n, n + 1))
    return found


@contextmanager
def phase(nc, kit, *names, gathers=0):
    with ExitStack() as st:
        kit.phases += 1
        sems = [st.enter_context(nc.semaphore(f"{n}_{kit.phases}")) for n in names]
        yield sems
        for numbers in runs([s.num for s in sems[:gathers]]):
            nc.gpsimd.dma_reset(numbers)
            nc.gpsimd.sem_clear(numbers)
        for numbers in runs([s.num for s in sems[gathers:]]):
            nc.sync.sem_clear(numbers)
        nc.all_engine_barrier()


def linker(eng, sem):
    count = [0]

    def link(ins):
        count[0] += 1
        ins.then_inc(sem, 1)
        eng.wait_ge(sem, count[0])

    return link


def setup(nc, kit):
    with phase(nc, kit, "const_in", "x_in") as (const_in, x_in):
        with nc.Block() as block:
            @block.sync
            def _(sp):
                sp.dma_start(kit.cst[:], kit.consts).then_inc(const_in, 16)
                sp.dma_start(kit.x_d[0:CTX, :], kit.ctx[0, :, :]).then_inc(x_in, 16)
                sp.dma_start(kit.x_d[CTX:T, :], kit.x[0, :, :]).then_inc(x_in, 16)
                sp.wait_ge(const_in, 16)
                sp.wait_ge(x_in, 32)

            @block.vector
            def _(dve):
                nc.vector.memset(kit.eps[:, 0:1], EPS)
                nc.vector.memset(kit.eps[:, 1:2], EPS * P)


def modulation(nc, kit, L):
    NCOL = 512
    NB = 6 * D // NCOL
    RING = 3
    with ExitStack() as mem, phase(nc, kit, "cond_in", "bias_in", "prm_in", "w0", "w1", "w2", "turned",
                                   "cond_ready", "prod_ready", "row_ready", "stored") as (
            cond_in, bias_in, prm_in, w0, w1, w2, turned, cond_ready, prod_ready, row_ready, stored):
        w_in = [w0, w1, w2]
        sb = lambda n, s: mem.enter_context(nc.sbuf_tensor(f"{n}_{L}", s, FP32))
        cond = sb("cond", [16, P])
        prm_rows = sb("prm_rows", [NPRM, P])
        condT = sb("condT", [P, KD, 2])
        wm = sb("wm", [P, RING, KD, NCOL])
        row = sb("modrow", [2, 6 * D])
        ps = kit.ps
        ident = kit.c("ident")

        with nc.Block() as block:
            @block.sync
            def _(sp):
                sp.dma_start(cond[0:8, :], kit.c_ctx.rearrange("(k p) -> k p", p=P)).then_inc(cond_in, 16)
                sp.dma_start(cond[8:16, :], kit.cnd[0, :].rearrange("(k p) -> k p", p=P)).then_inc(cond_in, 16)
                for i in range(2):
                    sp.dma_start(row[i:i + 1, :], kit.b_mod[L:L + 1, :]).then_inc(bias_in, 16)
                rows = [("conv", kit.conv_qkv[L].rearrange("t (c p) -> (t c) p", p=P), TAPS * NQKV),
                        ("dw", kit.dw_w[L].rearrange("t (c p) -> (t c) p", p=P), 2 * CONV_K),
                        ("dwb", kit.dw_b[L].rearrange("(c p) -> c p", p=P), 2),
                        ("gnw", kit.gn_w[L].rearrange("(c p) -> c p", p=P), 2),
                        ("gnb", kit.gn_b[L].rearrange("(c p) -> c p", p=P), 2)]
                for name, src, n in rows:
                    sp.dma_start(prm_rows[PRM[name]:PRM[name] + n, :], src).then_inc(prm_in, 16)
                for n in range(NB):
                    if n >= RING:
                        sp.wait_ge(prod_ready, n - RING + 1)
                    sp.dma_start(wm[:, n % RING, :, :],
                                 kit.w_mod[L, :, n * NCOL:(n + 1) * NCOL].rearrange("(k p) n -> p k n", p=P)
                                 ).then_inc(w_in[n % RING], 16)
                sp.wait_ge(row_ready, NB)
                sp.dma_start(kit.mod_d, row[:, :]).then_inc(stored, 16)
                sp.wait_ge(stored, 16)

            @block.tensor
            def _(pe):
                pe.wait_ge(cond_in, 32)
                nc.tensor.transpose(ps[:, 0, 0:16], cond[:, :], ident[0:16, 0:16]).then_inc(turned, 1)
                pe.wait_ge(prm_in, 80)
                nc.tensor.transpose(ps[:, 1, 0:NPRM], prm_rows[:, :], ident[0:NPRM, 0:NPRM]).then_inc(turned, 1)
                pe.wait_ge(cond_ready, 1)
                for n in range(NB):
                    pe.wait_ge(w_in[n % RING], 16 * (n // RING + 1))
                    if n >= 4:
                        pe.wait_ge(row_ready, n - 3)
                    for k in range(KD):
                        last = nc.tensor.matmul(ps[0:2, 2 + n % 4, 0:NCOL], condT[:, k, :], wm[:, n % RING, k, :],
                                                start=k == 0, stop=k == KD - 1)
                    last.then_inc(prod_ready, 1)

            @block.scalar
            def _(act):
                act.wait_ge(turned, 1)
                nc.scalar.activation(condT[:, :, :].rearrange("p k s -> p s k"),
                                     ps[:, 0, 0:16].rearrange("p (s k) -> p s k", s=2), ACT.Silu
                                     ).then_inc(cond_ready, 1)

            @block.vector
            def _(dve):
                dve.wait_ge(turned, 2)
                nc.vector.tensor_copy(kit.prm[:, :], ps[:, 1, 0:NPRM])
                dve.wait_ge(bias_in, 32)
                for n in range(NB):
                    dve.wait_ge(prod_ready, n + 1)
                    part = row[:, n * NCOL:(n + 1) * NCOL]
                    nc.vector.tensor_tensor(part, part, ps[0:2, 2 + n % 4, 0:NCOL], ALU.add).then_inc(row_ready, 1)


def mod_row(kit, stream, j):
    return kit.mod_d[stream:stream + 1, j * D:(j + 1) * D].broadcast_to([P, D])


def norm_in(nc, kit, L, hT):
    with ExitStack() as mem, phase(nc, kit, "rows_in", "x_in", "scale_ready", "ss_ready", "ms_ready",
                                   "root_ready", "h_ready", "turned", "hT_ready", "dve_step") as (
            rows_in, x_in, scale_ready, ss_ready, ms_ready, root_ready, h_ready, turned, hT_ready, dve_step):
        sb = lambda n, s: mem.enter_context(nc.sbuf_tensor(f"n1{n}_{L}", s, FP32))
        gain = sb("gain", [P, D])
        sc = sb("sc", [P, 2, D])
        sh = sb("sh", [P, 2, D])
        xb = sb("x", [P, NT, D])
        hb = sb("h", [P, 2, D])
        sq = sb("sq", [P, D])
        ss = sb("ss", [P, 3, NT])
        ps = kit.ps
        ident = kit.c("ident")

        with nc.Block() as block:
            @block.sync
            def _(sp):
                sp.dma_start(xb[:], kit.x_d.rearrange("(t p) n -> p t n", p=P)).then_inc(x_in, 16)
                sp.dma_start(gain[:], kit.norm1[L:L + 1, :].broadcast_to([P, D])).then_inc(rows_in, 16)
                for s in range(2):
                    sp.dma_start(sc[:, s, :], mod_row(kit, s, 1)).then_inc(rows_in, 16)
                    sp.dma_start(sh[:, s, :], mod_row(kit, s, 0)).then_inc(rows_in, 16)

            @block.scalar
            def _(act):
                act.wait_ge(x_in, 16)
                for t in range(NT):
                    if t:
                        act.wait_ge(ss_ready, t)
                    nc.scalar.activation(sq[:], xb[:, t, :], ACT.Square, accum_out=ss[:, 0, t:t + 1]
                                         ).then_inc(ss_ready, 1)
                act.wait_ge(ms_ready, 1)
                nc.scalar.activation(ss[:, 2, :], ss[:, 1, :], ACT.Sqrt).then_inc(root_ready, 1)
                for t in range(NT):
                    act.wait_ge(turned, t + 1)
                    b = 2 * (t % 2)
                    nc.scalar.activation(hT[:, :, t * P:(t + 1) * P],
                                         ps[:, b:b + 2, :].rearrange("p b (k n) -> p (b k) n", n=P),
                                         ACT.Copy).then_inc(hT_ready, 1)

            @block.vector
            def _(dve):
                link = linker(dve, dve_step)
                dve.wait_ge(rows_in, 80)
                for s in range(2):
                    link(nc.vector.scalar_tensor_tensor(out=sc[:, s, :], in0=sc[:, s, :], scalar=1.0,
                                                        in1=gain[:], op0=ALU.add, op1=ALU.mult))
                dve.wait_ge(ss_ready, NT)
                nc.vector.tensor_scalar(ss[:, 1, :], ss[:, 0, :], 1.0 / D, EPS, ALU.mult, ALU.add
                                        ).then_inc(ms_ready, 1)
                dve.wait_ge(root_ready, 1)
                link(nc.vector.reciprocal(ss[:, 0, :], ss[:, 2, :]))
                for t in range(NT):
                    s = int(t >= NC)
                    if t >= 2:
                        dve.wait_ge(turned, t - 1)
                    link(nc.vector.scalar_tensor_tensor(out=hb[:, t % 2, :], in0=xb[:, t, :],
                                                        scalar=ss[:, 0, t:t + 1], in1=sc[:, s, :],
                                                        op0=ALU.mult, op1=ALU.mult))
                    nc.vector.tensor_tensor(hb[:, t % 2, :], hb[:, t % 2, :], sh[:, s, :], ALU.add
                                            ).then_inc(h_ready, 1)

            @block.tensor
            def _(pe):
                for t in range(NT):
                    pe.wait_ge(h_ready, t + 1)
                    if t >= 2:
                        pe.wait_ge(hT_ready, t - 1)
                    for k in range(KD):
                        last = nc.tensor.transpose(ps[:, 2 * (t % 2) + k // 4, (k % 4) * P:(k % 4 + 1) * P],
                                                   hb[:, t % 2, k * P:(k + 1) * P], ident)
                    last.then_inc(turned, 1)


def projection(nc, kit, L, first, hT, qkvT, zs, ab, fT, acc):
    NCV, NFN = 4, 2
    chunks = ([C_OFF + c * P for c in range(NCV)] + [c * P for c in range(NQKV)]
              + [F_OFF + c * P for c in range(NFN)])
    whole = lambda c: first == 0 or NCV <= c < NCV + NQKV
    ROWS = SEQ // GRID_W
    W = GRID_W + 2 * HALO
    RING = 3
    NF = len(chunks)
    NU = 2 * H
    with ExitStack() as mem, phase(nc, kit, "w0", "w1", "w2", "wz_in", "proj_ready", "proj_read", "p_ready",
                                   "y_ready", "y_used", "rows_ready", "padded", "sq_ready", "sum_ready",
                                   "root_ready", "inverse_ready", "spread_ready", "unit_ready", "dve_step") as (
            w0, w1, w2, wz_in, proj_ready, proj_read, p_ready, y_ready, y_used, rows_ready, padded, sq_ready,
            sum_ready, root_ready, inverse_ready, spread_ready, unit_ready, dve_step):
        w_in = [w0, w1, w2]
        sb = lambda n, s: mem.enter_context(nc.sbuf_tensor(f"pj{n}_{L}", s, FP32))
        w = sb("w", [P, RING, KD, P])
        wz = kit.arena[:, 0:KD * GW].rearrange("p (k n) -> p k n", k=KD)
        sq = kit.arena[:, KD * GW:KD * GW + 2 * T].rearrange("p (c n) -> p c n", c=2)
        root = kit.arena[:, KD * GW + 2 * T:KD * GW + 3 * T]
        pick = kit.arena[:, KD * GW + 3 * T:KD * GW + 3 * T + 4 * NU].rearrange("p (s n) -> p s n", s=2)
        row_eps = kit.arena[:, KD * GW + 3 * T + 4 * NU:KD * GW + 3 * T + 4 * NU + 1]
        aT = kit.arena[:, KD * GW + 4 * T:KD * GW + 6 * T].rearrange("p (c n) -> p c n", c=2)
        gT = kit.arena[:, KD * GW + 6 * T:KD * GW + 8 * T].rearrange("p (c n) -> p c n", c=2)
        wab = sb("wab", [P, KD, 4 * H])
        spread = sb("spread", [NU, NU, P])
        pT = sb("p", [P, 2, T])
        yT = sb("y", [P, 2, T])
        lat = sb("lat", [P, 2, ROWS, W])
        ctx = sb("ctx", [P, 2, CTX + 2 * HALO])
        ps = kit.ps
        w_d = kit.w_in[L].rearrange("(k p) n -> p k n", p=P)

        with nc.Block() as block:
            @block.sync
            def _(sp):
                for c, off in enumerate(chunks):
                    if c >= RING:
                        sp.wait_ge(proj_ready, c - RING + 1)
                    sp.dma_start(w[:, c % RING, :, :], w_d[:, :, off:off + P]).then_inc(w_in[c % RING], 16)
                    if c == RING:
                        sp.dma_start(wz, w_d[:, :, Z_OFF:A_OFF]).then_inc(wz_in, 16)
                        sp.dma_start(wab[:], w_d[:, :, A_OFF:F_OFF]).then_inc(wz_in, 16)

            @block.tensor
            def _(pe):
                for c in range(NF):
                    pe.wait_ge(w_in[c % RING], 16 * (c // RING + 1))
                    if c >= 2:
                        pe.wait_ge(proj_read, c - 1)
                    b = 2 * (c % 2)
                    for k in range(KD):
                        last = nc.tensor.matmul(ps[:, b, 0:SEQ], w[:, c % RING, k, :], hT[:, k, CTX:T],
                                                start=k == 0, stop=k == KD - 1)
                    for k in range(KD if whole(c) else 0):
                        last = nc.tensor.matmul(ps[:, b + 1, 0:CTX], w[:, c % RING, k, :], hT[:, k, 0:CTX],
                                                start=k == 0, stop=k == KD - 1)
                    last.then_inc(proj_ready, 1)
                    q = c - NCV - 2
                    if 0 <= q < NU:
                        if q == 0:
                            pe.wait_ge(padded, 7)
                        pe.wait_ge(sq_ready, q + 1)
                        one = pick[:, int(q >= H), NU - 1 - q:2 * NU - 1 - q]
                        nc.tensor.matmul(ps[0:NU, 4, :], one, sq[:, q % 2, 0:512], start=q == 0, stop=q == NU - 1)
                        nc.tensor.matmul(ps[0:NU, 5, 0:T - 512], one, sq[:, q % 2, 512:T], start=q == 0,
                                         stop=q == NU - 1).then_inc(sum_ready, 1)
                pe.wait_ge(wz_in, 32)
                for t in range(NT):
                    if t == 1:
                        pe.wait_ge(root_ready, 1)
                    if t >= 2:
                        pe.wait_ge(rows_ready, t - 1)
                    for k in range(KD if t >= first else 0):
                        nc.tensor.matmul(ps[:, 6 - 2 * (t % 2), 0:GW], hT[:, k, t * P:(t + 1) * P], wz[:, k, :],
                                         start=k == 0, stop=k == KD - 1)
                    for k in range(KD):
                        last = nc.tensor.matmul(ps[:, 7 - 2 * (t % 2), 0:4 * H], hT[:, k, t * P:(t + 1) * P],
                                                wab[:, k, :], start=k == 0, stop=k == KD - 1)
                    last.then_inc(proj_ready, 1)
                    for q in range(2 * t - 2, min(2 * t, NU)) if t >= 1 else ():
                        if q == 0:
                            pe.wait_ge(inverse_ready, 1)
                            pe.wait_ge(proj_read, NF)
                        if q >= 2:
                            pe.wait_ge(unit_ready, q - 1)
                        b = 2 * (q % 2)
                        nc.tensor.matmul(ps[:, b, :], spread[:, q, :], root[0:NU, 0:512], start=True, stop=True)
                        nc.tensor.matmul(ps[:, b + 1, 0:T - 512], spread[:, q, :], root[0:NU, 512:T], start=True,
                                         stop=True).then_inc(spread_ready, 1)

            @block.scalar
            def _(act):
                def evacuate(c, out, func):
                    act.wait_ge(proj_ready, c + 1)
                    b = 2 * (c % 2)
                    if whole(c):
                        nc.scalar.activation(out[:, 0:CTX], ps[:, b + 1, 0:CTX], func)
                    nc.scalar.activation(out[:, CTX:T], ps[:, b, 0:SEQ], func).then_inc(proj_read, 1)

                def silu(c):
                    act.wait_ge(y_ready, c + 1)
                    nc.scalar.activation(qkvT[:, c, :], yT[:, c % 2, :], ACT.Silu).then_inc(y_used, 1)

                def square(c):
                    act.wait_ge(y_used, c + 1)
                    if c >= 2:
                        act.wait_ge(sum_ready, c - 1)
                    nc.scalar.activation(sq[:, c % 2, :], qkvT[:, c, :], ACT.Square).then_inc(sq_ready, 1)

                def lengths():
                    act.wait_ge(sum_ready, NU)
                    act.wait_ge(padded, 7)
                    nc.scalar.activation(root[0:NU, 0:512], ps[0:NU, 4, :], ACT.Sqrt, bias=row_eps[0:NU, :])
                    nc.scalar.activation(root[0:NU, 512:T], ps[0:NU, 5, 0:T - 512], ACT.Sqrt,
                                         bias=row_eps[0:NU, :]).then_inc(root_ready, 1)

                for i in range(2):
                    evacuate(i, aT[:, i, :], ACT.Copy)
                for i in range(2):
                    evacuate(2 + i, gT[:, i, :], ACT.Sigmoid)
                for c in range(NQKV):
                    if c >= 2:
                        act.wait_ge(y_ready, c - 1)
                    evacuate(NCV + c, pT[:, c % 2, :], ACT.Copy)
                    if c >= 1:
                        silu(c - 1)
                    if 0 <= c - 1 < NU:
                        square(c - 1)
                silu(NQKV - 1)
                lengths()
                for i in range(NFN):
                    evacuate(NCV + NQKV + i, fT[:, i, :], ACT.Copy)
                for t in range(NT):
                    act.wait_ge(proj_ready, NF + t + 1)
                    if t >= first:
                        nc.scalar.activation(zs[:, t, :], ps[:, 6 - 2 * (t % 2), 0:GW], ACT.Silu)
                    nc.scalar.activation(ab[:, t, :], ps[:, 7 - 2 * (t % 2), 0:4 * H], ACT.Copy
                                         ).then_inc(rows_ready, 1)

            @block.vector
            def _(dve):
                link = linker(dve, dve_step)
                def pad(c):
                    dve.wait_ge(padded, 2)
                    dve.wait_ge(proj_read, NCV)
                    link(nc.vector.tensor_tensor(lat[:, c, :, HALO:HALO + GRID_W],
                                                 aT[:, c, CTX:T].rearrange("p (r w) -> p r w", w=GRID_W),
                                                 gT[:, c, CTX:T].rearrange("p (r w) -> p r w", w=GRID_W), ALU.mult))
                    if first == 0:
                        link(nc.vector.tensor_tensor(ctx[:, c, HALO:HALO + CTX], aT[:, c, 0:CTX], gT[:, c, 0:CTX],
                                                     ALU.mult))

                def tap_rows(c, j):
                    tap = kit.prm[:, PRM["dw"] + 2 * j + c:PRM["dw"] + 2 * j + c + 1]
                    bias = kit.prm[:, PRM["dwb"] + c:PRM["dwb"] + c + 1]
                    rows = [(acc[:, c, CTX:T].rearrange("p (r w) -> p r w", w=GRID_W), lat[:, c, :, j:j + GRID_W])]
                    if first == 0:
                        rows.append((acc[:, c, 0:CTX], ctx[:, c, j:j + CTX]))
                    for out, src in rows:
                        if j == 0:
                            link(nc.vector.tensor_scalar(out, src, tap, bias, ALU.mult, ALU.add))
                        else:
                            link(nc.vector.scalar_tensor_tensor(out=out, in0=src, scalar=tap, in1=out,
                                                                op0=ALU.mult, op1=ALU.add))

                for q in range(NU):
                    last = nc.vector.tensor_scalar(spread[:, q, :], kit.c("ones")[0:NU, :],
                                                   kit.c("ident")[0:NU, q:q + 1], None, ALU.mult)
                link(last)
                TAPS_EACH = -(-2 * CONV_K // NQKV)
                for c in range(NQKV):
                    tap = lambda j: kit.prm[:, PRM["conv"] + j * NQKV + c:PRM["conv"] + j * NQKV + c + 1]
                    p, y = pT[:, c % 2, :], yT[:, c % 2, :]
                    dve.wait_ge(proj_read, NCV + c + 1)
                    if c >= 2:
                        dve.wait_ge(y_used, c - 1)
                    link(nc.vector.tensor_scalar(y, p, tap(1), None, ALU.mult))
                    for a, b in ((0, CTX), (CTX, T)):
                        link(nc.vector.scalar_tensor_tensor(out=y[:, a + 1:b], in0=p[:, a:b - 1], scalar=tap(0),
                                                            in1=y[:, a + 1:b], op0=ALU.mult, op1=ALU.add))
                    for a, b in ((0, CTX), (CTX, T)):
                        last = nc.vector.scalar_tensor_tensor(out=y[:, a:b - 1], in0=p[:, a + 1:b], scalar=tap(2),
                                                              in1=y[:, a:b - 1], op0=ALU.mult, op1=ALU.add)
                        if a == 0:
                            link(last)
                    last.then_inc(y_ready, 1)
                    for n in range(c * TAPS_EACH, min((c + 1) * TAPS_EACH, 2 * CONV_K)):
                        if n % CONV_K == 0:
                            pad(n // CONV_K)
                        tap_rows(n // CONV_K, n % CONV_K)
                dve.wait_ge(root_ready, 1)
                nc.vector.reciprocal(root[0:NU, :], root[0:NU, :]).then_inc(inverse_ready, 1)
                for q in range(NU):
                    dve.wait_ge(spread_ready, q + 1)
                    b = 2 * (q % 2)
                    nc.vector.tensor_tensor(qkvT[:, q, 0:512], qkvT[:, q, 0:512], ps[:, b, :], ALU.mult)
                    nc.vector.tensor_tensor(qkvT[:, q, 512:T], qkvT[:, q, 512:T], ps[:, b + 1, 0:T - 512],
                                            ALU.mult).then_inc(unit_ready, 1)

            @block.gpsimd
            def _(pool):
                nc.gpsimd.memset(lat[:], 0.0).then_inc(padded, 1)
                nc.gpsimd.memset(ctx[:], 0.0).then_inc(padded, 1)
                nc.gpsimd.memset(pick, 0.0).then_inc(padded, 1)
                nc.gpsimd.memset(row_eps[0:NU, :], EPS).then_inc(padded, 1)
                pool.wait_ge(padded, 4)
                nc.gpsimd.memset(pick[:, 0, NU - 1:NU], float(P)).then_inc(padded, 1)
                nc.gpsimd.memset(pick[:, 1, NU - 1:NU], 1.0).then_inc(padded, 1)
                nc.gpsimd.memset(row_eps[0:H, :], EPS * P).then_inc(padded, 1)


def branches(nc, kit, L, first, fT, acc, mixT, ab, gate):
    G = 2 * H
    segs = [(CTX, SEQ, 4, 0), (0, CTX, 2, 1)]
    if first:
        segs = segs[:1]
    with ExitStack() as mem, phase(nc, kit, "rows_in", "e_alog", "arg_ready", "exp_ready", "dft_in", "mean_ready",
                                   "cent_ready", "sq_ready", "var_ready", "root_ready", "norm_ready",
                                   "half_ready", "half_read", "seq_ready", "dve_step") as (
            rows_in, e_alog, arg_ready, exp_ready, dft_in, mean_ready, cent_ready, sq_ready, var_ready, root_ready,
            norm_ready, half_ready, half_read, seq_ready, dve_step):
        sb = lambda n, s: mem.enter_context(nc.sbuf_tensor(f"cf{n}_{L}", s, FP32))
        sq = sb("sq", [P, 2, T])
        dft_l = sb("dftl", [P, 4, 2, SEQ])
        dft_c = sb("dftc", [P, 2, 2, CTX])
        half = sb("half", [P, NT, 2, 2, P])
        alog = sb("alog", [P, G])
        dt = sb("dt", [P, G])
        v = sb("v", [P, 8, NT, G])
        ps = kit.ps
        tables = [dft_l, dft_c]

        cols = [(slice(s[0], s[0] + s[1]), b, s[1]) for b, s in enumerate(segs)]
        every = slice(0 if first == 0 else CTX, T)

        with nc.Block() as block:
            @block.sync
            def _(sp):
                sp.dma_start(alog[:], kit.a_log[L:L + 1].rearrange("l d h -> l (d h)").broadcast_to([P, G])
                             ).then_inc(rows_in, 16)
                sp.dma_start(dt[:], kit.dt_bias[L:L + 1].rearrange("l d h -> l (d h)").broadcast_to([P, G])
                             ).then_inc(rows_in, 16)
                for s in range(2):
                    sp.dma_start(dft_l[:, :, s, :], kit.dft_l[s].rearrange("(t p) n -> p t n", p=P)
                                 ).then_inc(dft_in, 16)
                    sp.dma_start(dft_c[:, :, s, :], kit.dft_c[s].rearrange("(t p) n -> p t n", p=P)
                                 ).then_inc(dft_in, 16)

            @block.vector
            def _(dve):
                link = linker(dve, dve_step)
                wide = lambda a: a[:, None, :].to_broadcast([P, NT, G])
                dve.wait_ge(rows_in, 32)
                link(nc.vector.tensor_tensor(v[:, 0], ab[:, :, 0:G], wide(dt[:]), ALU.add))
                link(nc.vector.tensor_scalar(v[:, 3], v[:, 0], -1.0, None, ALU.mult))
                nc.vector.tensor_tensor(v[:, 1], v[:, 0], v[:, 3], ALU.max).then_inc(arg_ready, 1)
                dve.wait_ge(exp_ready, 2)
                link(nc.vector.tensor_scalar(v[:, 3], v[:, 2], 2.0, None, ALU.add))
                link(nc.vector.reciprocal(v[:, 4], v[:, 3]))
                link(nc.vector.tensor_tensor(v[:, 5], v[:, 2], v[:, 4], ALU.mult))
                link(nc.vector.tensor_tensor(v[:, 6], v[:, 5], v[:, 5], ALU.mult))
                link(nc.vector.tensor_scalar(v[:, 7], v[:, 6], 1.0 / 17, 1.0 / 15, ALU.mult, ALU.add))
                for n in (13, 11, 9, 7, 5, 3, 1):
                    link(nc.vector.tensor_tensor(v[:, 7], v[:, 7], v[:, 6], ALU.mult))
                    link(nc.vector.tensor_scalar(v[:, 7], v[:, 7], 1.0 / n, None, ALU.add))
                link(nc.vector.scalar_tensor_tensor(out=v[:, 7], in0=v[:, 7], scalar=2.0, in1=v[:, 5],
                                                    op0=ALU.mult, op1=ALU.mult))
                link(nc.vector.scalar_tensor_tensor(out=v[:, 7], in0=v[:, 0], scalar=0.0, in1=v[:, 7],
                                                    op0=ALU.max, op1=ALU.add))
                dve.wait_ge(e_alog, 1)
                nc.vector.scalar_tensor_tensor(out=gate[:, :, 0:G], in0=v[:, 7], scalar=-1.0, in1=wide(alog[:]),
                                               op0=ALU.mult, op1=ALU.mult)
                for c in range(2):
                    dve.wait_ge(mean_ready, c + 1)
                    for col, b, size in cols:
                        last = nc.vector.tensor_tensor(acc[:, c, col], acc[:, c, col], ps[:, b, 0:size],
                                                       ALU.subtract)
                        if b < len(cols) - 1:
                            link(last)
                    last.then_inc(cent_ready, 1)
                    dve.wait_ge(root_ready, c + 1)
                    link(nc.vector.reciprocal(sq[:, c, every], sq[:, c, every]))
                    nc.vector.tensor_tensor(acc[:, c, every], acc[:, c, every], sq[:, c, every], ALU.mult
                                            ).then_inc(norm_ready, 1)

            @block.scalar
            def _(act):
                act.wait_ge(rows_in, 32)
                nc.scalar.activation(alog[:], alog[:], ACT.Exp).then_inc(e_alog, 1)
                act.wait_ge(arg_ready, 1)
                nc.scalar.activation(v[:, 2], v[:, 1], ACT.Exp, scale=-1.0).then_inc(exp_ready, 1)
                nc.scalar.activation(gate[:, :, G:2 * G], ab[:, :, G:2 * G], ACT.Sigmoid).then_inc(exp_ready, 1)
                n = 0
                for t in range(first, NT):
                    for c in range(2):
                        act.wait_ge(half_ready, n + 1)
                        nc.scalar.activation(half[:, t, c].rearrange("p s n -> p (s n)"), ps[:, 4 + n % 2, 0:2 * P],
                                             ACT.Copy).then_inc(half_read, 1)
                        n += 1
                n = 0
                for base, rows, tiles, tab in segs:
                    for c in range(2):
                        act.wait_ge(seq_ready, n + 1)
                        nc.scalar.activation(mixT[:, 4 + c, base:base + rows], ps[:, 6 + n % 2, 0:rows],
                                             ACT.Copy).then_inc(half_read, 1)
                        n += 1
                for c in range(2):
                    act.wait_ge(cent_ready, c + 1)
                    nc.scalar.activation(sq[:, c, every], acc[:, c, every], ACT.Square).then_inc(sq_ready, 1)
                    act.wait_ge(var_ready, c + 1)
                    for col, b, size in cols:
                        last = nc.scalar.activation(sq[:, c, col], ps[:, 2 + b, 0:size], ACT.Sqrt,
                                                    bias=kit.eps[:, 0:1])
                    last.then_inc(root_ready, 1)
                    act.wait_ge(norm_ready, c + 1)
                    nc.scalar.activation(mixT[:, 6 + c, every], acc[:, c, every], ACT.Silu,
                                         bias=kit.prm[:, PRM["gnb"] + c:PRM["gnb"] + c + 1],
                                         scale=kit.prm[:, PRM["gnw"] + c:PRM["gnw"] + c + 1])

            @block.tensor
            def _(pe):
                n = 0
                for t in range(first, NT):
                    for c in range(2):
                        if n >= 2:
                            pe.wait_ge(half_read, n - 1)
                        nc.tensor.matmul(ps[:, 4 + n % 2, 0:2 * P], fT[:, c, t * P:(t + 1) * P],
                                         kit.c2("C64"), start=True, stop=True).then_inc(half_ready, 1)
                        n += 1
                pe.wait_ge(dft_in, 64)
                pe.wait_ge(half_read, n)
                m = 0
                for base, rows, tiles, tab in segs:
                    for c in range(2):
                        if m >= 2:
                            pe.wait_ge(half_read, n + m - 1)
                        for i in range(tiles):
                            for s in range(2):
                                last = nc.tensor.matmul(ps[:, 6 + m % 2, 0:rows], half[:, base // P + i, c, s, :],
                                                        tables[tab][:, i, s, :], start=(i, s) == (0, 0),
                                                        stop=(i, s) == (tiles - 1, 1))
                        last.then_inc(seq_ready, 1)
                        m += 1
                for c in range(2):
                    if c:
                        pe.wait_ge(cent_ready, c)
                    for col, b, size in cols:
                        last = nc.tensor.matmul(ps[:, b, 0:size], kit.c("gmean"), acc[:, c, col],
                                                start=True, stop=True)
                    last.then_inc(mean_ready, 1)
                    pe.wait_ge(sq_ready, c + 1)
                    for col, b, size in cols:
                        last = nc.tensor.matmul(ps[:, 2 + b, 0:size], kit.c("gmean"), sq[:, c, col],
                                                start=True, stop=True)
                    last.then_inc(var_ready, 1)


def gdn_tiles(nc, kit, L, qkvT, gate, kt, u, wT, qkd, dec):
    G = 2 * H
    NL = len(LEVELS) - 1
    with ExitStack() as mem, phase(
            nc, kit, "rows_turned", "rows_ready", "gram_ready", "gram_used", "sums_ready", "dec_ready",
            "gmask_ready", "diff_ready", "exp_ready", "a_ready", "qk_ready", "block_ready", "inv1_ready",
            "inv1_turned", "invT1_ready", "w_ready", "w_copied", "upd_ready", "upd_done", "rhs_ready",
            "uw_ready", "uw_copied", "dve_step", "pool_step") as (
            rows_turned, rows_ready, gram_ready, gram_used, sums_ready, dec_ready,
            gmask_ready, diff_ready, exp_ready, a_ready, qk_ready, block_ready, inv1_ready,
            inv1_turned, invT1_ready, w_ready, w_copied, upd_ready, upd_done, rhs_ready,
            uw_ready, uw_copied, dve_step, pool_step):
        sb = lambda n, s: mem.enter_context(nc.sbuf_tensor(f"gd{n}_{L}", s, FP32))
        ra = sb("ra", [P, 2, 2, H, P])
        rb = sb("rb", [P, 2, H, P])
        w = sb("w", [P, 2, H, P])
        inv = sb("inv", [P, 2, H, P])
        invT = sb("invT", [P, 2, H, P])
        blk = sb("blk", [P, 2, H, P])
        vt = sb("vt", [P, H, P])
        bg = sb("bg", [P, 2, H])
        ps = kit.ps
        ident = kit.c("ident")
        wide = lambda a: a[:, :, None].to_broadcast([P, H, P])
        heads = lambda a: a[:, None, :].to_broadcast([P, H, P])
        flat = lambda a: a.rearrange("p h n -> p (h n)")
        bank = lambda b: ps[:, b, :].rearrange("p (h n) -> p h n", h=H)
        last_level = lambda t, d: 2 * NL * t + 2 * (NL - 1) + d + 1

        with nc.Block() as block:
            @block.tensor
            def _(pe):
                def turn_rows(t):
                    tok = slice(t * P, (t + 1) * P)
                    if t:
                        pe.wait_ge(exp_ready, 2 * t)
                    for h in range(H):
                        nc.tensor.transpose(bank(0)[:, h, :], qkvT[:, H + h, tok], ident)
                    for h in range(H):
                        last = nc.tensor.transpose(bank(1)[:, h, :], qkvT[:, 2 * H + h, tok], ident)
                    last.then_inc(rows_turned, 1)
                    if t:
                        pe.wait_ge(gram_used, 2 * t)
                    for h in range(H):
                        nc.tensor.matmul(bank(2)[:, h, :], qkvT[:, H + h, tok], qkvT[:, H + h, tok],
                                         start=True, stop=True)
                    for h in range(H):
                        last = nc.tensor.matmul(bank(3)[:, h, :], qkvT[:, H + h, tok], qkvT[:, h, tok],
                                                start=True, stop=True)
                    last.then_inc(gram_ready, 1)

                def sums(t):
                    pe.wait_ge(rows_ready, t + 1)
                    for d in range(2):
                        for kind, m in enumerate((f"L{d}", f"M{d}", "CH0", "CH1")):
                            col = (4 * d + kind) * H
                            last = nc.tensor.matmul(ps[:, 0, col:col + H], kit.c(m), gate[:, t, d * H:(d + 1) * H],
                                                    start=True, stop=True)
                    last.then_inc(sums_ready, 1)

                def differences(t, d):
                    if d == 0:
                        pe.wait_ge(dec_ready, t + 1)
                    else:
                        pe.wait_ge(exp_ready, 2 * t + 1)
                    pe.wait_ge(gmask_ready, 2 * t + d + 1)
                    nc.tensor.matmul(ps[:, 0, :], kit.c(f"L{d}"), flat(ra[:, t % 2, d]), start=True, stop=True)
                    nc.tensor.matmul(ps[:, 1, :], kit.c(f"M{d}"), flat(rb[:, d]), start=True, stop=True
                                     ).then_inc(diff_ready, 1)

                turn_rows(0)
                sums(0)
                differences(0, 0)
                differences(0, 1)
                for t in range(NT):
                    if t:
                        pe.wait_ge(uw_copied, 2 * t)
                    for d in range(2):
                        pe.wait_ge(inv1_ready, 2 * t + d + 1)
                        for h in range(H):
                            last = nc.tensor.transpose(bank(5 + 2 * d)[:, h, :], inv[:, d, h, :], ident)
                        last.then_inc(inv1_turned, 1)
                    for n in range(NL):
                        for d in range(2):
                            m = 2 * NL * t + 2 * n + d
                            pe.wait_ge(block_ready, 2 * (NL + 1) * t + 2 * (n + 1) + d + 1)
                            if n == 0:
                                pe.wait_ge(invT1_ready, 2 * t + d + 1)
                            else:
                                pe.wait_ge(upd_done, m - 1)
                            for h in range(H):
                                last = nc.tensor.matmul(bank(4 + 2 * d)[:, h, :], blk[:, d, h, :], invT[:, d, h, :],
                                                        start=True, stop=True)
                            last.then_inc(w_ready, 1)
                        for d in range(2):
                            pe.wait_ge(w_copied, 2 * NL * t + 2 * n + d + 1)
                            for h in range(H):
                                last = nc.tensor.matmul(bank(5 + 2 * d)[:, h, :], inv[:, d, h, :], w[:, d, h, :],
                                                        start=True, stop=True)
                            if n < NL - 1:
                                for h in range(H):
                                    last = nc.tensor.matmul(bank(4 + 2 * d)[:, h, :], w[:, d, h, :], inv[:, d, h, :],
                                                            start=True, stop=True)
                            last.then_inc(upd_ready, 1)
                        if t + 1 < NT:
                            if n == 0:
                                turn_rows(t + 1)
                            elif n == 1:
                                sums(t + 1)
                            elif n < 4:
                                differences(t + 1, n - 2)
                    for d in range(2):
                        pe.wait_ge(upd_done, last_level(t, d))
                        pe.wait_ge(rhs_ready, 2 * t + d + 1)
                        for h in range(H):
                            nc.tensor.matmul(bank(5 + 2 * d)[:, h, :], invT[:, d, h, :], u[:, d, t, h, :],
                                             start=True, stop=True)
                        for h in range(H):
                            last = nc.tensor.matmul(bank(4 + 2 * d)[:, h, :], wT[:, d, t, h, :], invT[:, d, h, :],
                                                    start=True, stop=True)
                        last.then_inc(uw_ready, 1)

            @block.scalar
            def _(act):
                def copy_rows(t):
                    act.wait_ge(rows_turned, t + 1)
                    nc.scalar.activation(kt[:, t], bank(0), ACT.Copy)
                    if t:
                        act.wait_ge(rhs_ready, 2 * t)
                    nc.scalar.activation(vt[:], bank(1), ACT.Copy).then_inc(rows_ready, 1)

                def decays(t):
                    act.wait_ge(sums_ready, t + 1)
                    nc.scalar.activation(dec[:, t].rearrange("p d k h -> p (d k h)"), ps[:, 0, 0:8 * H], ACT.Exp
                                         ).then_inc(dec_ready, 1)

                def decay_matrices(t, d):
                    act.wait_ge(diff_ready, 2 * t + d + 1)
                    nc.scalar.activation(ra[:, t % 2, d], bank(0), ACT.Exp)
                    nc.scalar.activation(rb[:, d], bank(1), ACT.Exp).then_inc(exp_ready, 1)

                copy_rows(0)
                decays(0)
                decay_matrices(0, 0)
                decay_matrices(0, 1)
                for t in range(NT):
                    for d in range(2):
                        act.wait_ge(inv1_turned, 2 * t + d + 1)
                        nc.scalar.activation(invT[:, d], bank(5 + 2 * d), ACT.Copy).then_inc(invT1_ready, 1)
                    for n in range(NL):
                        for d in range(2):
                            act.wait_ge(w_ready, 2 * NL * t + 2 * n + d + 1)
                            nc.scalar.activation(w[:, d], bank(4 + 2 * d), ACT.Copy).then_inc(w_copied, 1)
                        if t + 1 < NT:
                            if n == 0:
                                copy_rows(t + 1)
                            elif n == 1:
                                decays(t + 1)
                            elif n < 4:
                                decay_matrices(t + 1, n - 2)
                    for d in range(2):
                        act.wait_ge(uw_ready, 2 * t + d + 1)
                        nc.scalar.activation(u[:, d, t], bank(5 + 2 * d), ACT.Copy)
                        nc.scalar.activation(wT[:, d, t], bank(4 + 2 * d), ACT.Copy).then_inc(uw_copied, 1)

            @block.vector
            def _(dve):
                link = linker(dve, dve_step)

                def system(t, d):
                    beta = gate[:, t, G + d * H:G + (d + 1) * H]
                    A = ra[:, t % 2, d]
                    dve.wait_ge(gram_ready, t + 1)
                    dve.wait_ge(exp_ready, 2 * t + d + 1)
                    link(nc.vector.tensor_tensor(A, A, bank(2), ALU.mult))
                    nc.vector.tensor_tensor(A, A, wide(beta), ALU.mult).then_inc(a_ready, 1)
                    nc.vector.tensor_tensor(qkd[:, d, t], rb[:, d], bank(3), ALU.mult).then_inc(gram_used, 1)
                    dve.wait_ge(gram_used, 2 * t + d + 1)
                    nc.vector.tensor_tensor(qkd[:, d, t], qkd[:, d, t], heads(kit.c(f"L{d}")), ALU.mult
                                            ).then_inc(qk_ready, 1)

                system(0, 0)
                system(0, 1)
                for t in range(NT):
                    for d in range(2):
                        dve.wait_ge(block_ready, 2 * (NL + 1) * t + d + 1)
                        nc.vector.tensor_tensor(inv[:, d], heads(ident), blk[:, d], ALU.subtract
                                                ).then_inc(inv1_ready, 1)
                    for n in range(NL):
                        for d in range(2):
                            dve.wait_ge(upd_ready, 2 * NL * t + 2 * n + d + 1)
                            op = nc.vector.tensor_tensor(invT[:, d], invT[:, d], bank(5 + 2 * d), ALU.subtract)
                            if n < NL - 1:
                                op = nc.vector.tensor_tensor(inv[:, d], inv[:, d], bank(4 + 2 * d), ALU.subtract)
                            op.then_inc(upd_done, 1)
                        if t + 1 < NT and n >= NL - 2:
                            system(t + 1, n - (NL - 2))

            @block.gpsimd
            def _(pool):
                link = linker(pool, pool_step)

                def mask_gates(t):
                    for d in range(2):
                        if t:
                            pool.wait_ge(qk_ready, 2 * (t - 1) + d + 1)
                        g = gate[:, t, d * H:(d + 1) * H]
                        link(nc.gpsimd.tensor_tensor(ra[:, t % 2, d], heads(kit.c(f"M{d}")), wide(g), ALU.mult))
                        nc.gpsimd.tensor_tensor(rb[:, d], heads(kit.c(f"L{d}")), wide(g), ALU.mult
                                                ).then_inc(gmask_ready, 1)

                def right_sides(t):
                    pool.wait_ge(rows_ready, t + 1)
                    pool.wait_ge(dec_ready, t + 1)
                    for d in range(2):
                        beta = gate[:, t, G + d * H:G + (d + 1) * H]
                        link(nc.gpsimd.tensor_tensor(u[:, d, t], vt[:], wide(beta), ALU.mult))
                        link(nc.gpsimd.tensor_tensor(bg[:, d], dec[:, t, d, 0, :], beta, ALU.mult))
                        nc.gpsimd.tensor_tensor(wT[:, d, t], kt[:, t], wide(bg[:, d]), ALU.mult
                                                ).then_inc(rhs_ready, 1)

                mask_gates(0)
                right_sides(0)
                for t in range(NT):
                    for n in range(NL + 1):
                        for d in range(2):
                            if n == 0:
                                pool.wait_ge(a_ready, 2 * t + d + 1)
                                if t:
                                    pool.wait_ge(w_ready, last_level(t - 1, d))
                            elif n == 1:
                                pool.wait_ge(inv1_ready, 2 * t + d + 1)
                            else:
                                pool.wait_ge(w_ready, 2 * NL * t + 2 * (n - 2) + d + 1)
                            nc.gpsimd.tensor_tensor(blk[:, d], ra[:, t % 2, d], heads(kit.c(f"B{d}_{n}")), ALU.mult
                                                    ).then_inc(block_ready, 1)
                        if t + 1 < NT:
                            if n == 2:
                                mask_gates(t + 1)
                            elif n == 4:
                                right_sides(t + 1)


def gdn_scan(nc, kit, L, qkvT, kt, u, wT, qkd, dec, o):
    NCH = T // CHUNK
    CC = CTX // CHUNK
    with ExitStack() as mem, phase(nc, kit, "zeroed", "v_ready", "s_ready", "vo_ready", "vnew_ready", "os_ready", "state_ready",
                                   "tail_ready", "decayed", "o_ready", "dve_step") as (
            zeroed, v_ready, s_ready, vo_ready, vnew_ready, os_ready, state_ready, tail_ready, decayed, o_ready, dve_step):
        sb = lambda n, s: mem.enter_context(nc.sbuf_tensor(f"sc{n}_{L}", s, FP32))
        S = sb("S", [P, 2, H, P])
        Sd = sb("Sd", [P, 2, H, P])
        vn = sb("vn", [P, 2, H, P])
        tail = sb("tail", [P, 2, H, P])
        part = sb("part", [P, 2, H, P])
        ps = kit.ps
        bank = lambda b: ps[:, b, :].rearrange("p (h n) -> p h n", h=H)

        def place(s, d):
            c = s if d == 0 else (CC - 1 - s if s < CC else NCH - 1 + CC - s)
            return c // 2, c % 2, slice(CHUNK * (c % 2), CHUNK * (c % 2 + 1))

        with nc.Block() as block:
            @block.tensor
            def _(pe):
                pe.wait_ge(zeroed, 2)
                for s in range(NCH):
                    for d in range(2):
                        t, half, R = place(s, d)
                        if s:
                            pe.wait_ge(state_ready, 2 * (s - 1) + d + 1)
                        for h in range(H):
                            last = nc.tensor.matmul(bank(4 * d)[R, h, :], wT[:, d, t, h, R], S[:, d, h, :],
                                                    start=True, stop=True)
                        last.then_inc(v_ready, 1)
                    for d in range(2):
                        t, half, R = place(s, d)
                        tok = slice(t * P + R.start, t * P + R.stop)
                        for h in range(H):
                            last = nc.tensor.matmul(bank(4 * d + 1)[R, h, :], qkvT[:, h, tok], S[:, d, h, :],
                                                    start=True, stop=True)
                        last.then_inc(vo_ready, 1)
                    for d in range(2):
                        pe.wait_ge(vnew_ready, 2 * s + d + 1)
                        pe.wait_ge(tail_ready, 2 * s + d + 1)
                        t, half, R = place(s, d)
                        for h in range(H):
                            last = nc.tensor.matmul(bank(4 * d + 3)[:, h, :], tail[R, d, h, :], vn[R, d, h, :],
                                                    start=True, stop=True)
                        last.then_inc(s_ready, 1)
                    for d in range(2):
                        t, half, R = place(s, d)
                        if s:
                            pe.wait_ge(o_ready, 2 * (s - 1) + d + 1)
                        for h in range(H):
                            last = nc.tensor.matmul(bank(4 * d + 2)[R, h, :], qkd[R, d, t, h, R], vn[R, d, h, :],
                                                    start=True, stop=True)
                        last.then_inc(os_ready, 1)

            @block.vector
            def _(dve):
                link = linker(dve, dve_step)
                nc.vector.memset(S[:], 0.0).then_inc(zeroed, 1)
                nc.vector.memset(o[:], 0.0).then_inc(zeroed, 1)
                for s in range(NCH):
                    for d in range(2):
                        t, half, R = place(s, d)
                        dve.wait_ge(v_ready, 2 * s + d + 1)
                        if s:
                            dve.wait_ge(os_ready, 2 * (s - 1) + d + 1)
                        nc.vector.tensor_tensor(vn[R, d], u[R, d, t], bank(4 * d)[R], ALU.subtract
                                                ).then_inc(vnew_ready, 1)
                    for d in range(2):
                        t, half, R = place(s, d)
                        dve.wait_ge(vo_ready, 2 * s + d + 1)
                        link(nc.vector.tensor_tensor(part[R, d], bank(4 * d + 1)[R],
                                                     dec[R, t, d, 0, :][:, :, None].to_broadcast([CHUNK, H, P]),
                                                     ALU.mult))
                    for d in range(2):
                        dve.wait_ge(s_ready, 2 * s + d + 1)
                        dve.wait_ge(decayed, 2 * s + d + 1)
                        nc.vector.tensor_tensor(S[:, d], Sd[:, d], bank(4 * d + 3), ALU.add
                                                ).then_inc(state_ready, 1)
                    for d in range(2):
                        t, half, R = place(s, d)
                        link(nc.vector.tensor_tensor(o[R, t], o[R, t], part[R, d], ALU.add))
                        dve.wait_ge(os_ready, 2 * s + d + 1)
                        nc.vector.tensor_tensor(o[R, t], o[R, t], bank(4 * d + 2)[R], ALU.add
                                                ).then_inc(o_ready, 1)
                        dve.wait_ge(o_ready, 2 * s + d + 1)

            @block.gpsimd
            def _(pool):
                pool.wait_ge(zeroed, 2)
                for s in range(NCH):
                    for d in range(2):
                        t, half, R = place(s, d)
                        if s:
                            pool.wait_ge(os_ready, 2 * (s - 1) + d + 1)
                        nc.gpsimd.tensor_tensor(tail[R, d], kt[R, t],
                                                dec[R, t, d, 1, :][:, :, None].to_broadcast([CHUNK, H, P]),
                                                ALU.mult).then_inc(tail_ready, 1)
                        pool.wait_ge(tail_ready, 2 * s + d + 1)
                        if s:
                            pool.wait_ge(state_ready, 2 * (s - 1) + d + 1)
                        nc.gpsimd.tensor_tensor(Sd[:, d], S[:, d],
                                                dec[:, t, d, 2 + half, :][:, :, None].to_broadcast([P, H, P]),
                                                ALU.mult).then_inc(decayed, 1)
                        pool.wait_ge(decayed, 2 * s + d + 1)


def gdn_out(nc, kit, L, first, o, zs, mixT, w_out, w_arrived, wq_in):
    with ExitStack() as mem, phase(nc, kit, "gain_in", "ms_ready", "root_ready", "y_ready", "turned", "copied",
                                   "dve_step") as (
            gain_in, ms_ready, root_ready, y_ready, turned, copied, dve_step):
        sb = lambda n, s: mem.enter_context(nc.sbuf_tensor(f"go{n}_{L}", s, FP32))
        gain = sb("gain", [P, P])
        sq = sb("sq", [P, (NT - first) * H, P])
        ss = sb("ss", [P, 2, (NT - first) * H])
        ps = kit.ps
        y = o[:, first:].rearrange("p t h n -> p (t h) n")
        N = (NT - first) * H

        with nc.Block() as block:
            @block.sync
            def _(sp):
                sp.dma_start(gain[:], kit.gdn_norm[L:L + 1, :].broadcast_to([P, P])).then_inc(gain_in, 16)
                sp.dma_start(w_out[:], kit.w_out[L].rearrange("(k p) n -> p k n", p=P)).then_inc(w_arrived, 16)
                for b in range(2):
                    sp.dma_start(kit.wq[:, b * KD // 2:(b + 1) * KD // 2, :],
                                 kit.peer_wq[L, b * D // 2:(b + 1) * D // 2, :].rearrange("(k p) n -> p k n", p=P)
                                 ).then_inc(wq_in, 16)

            @block.vector
            def _(dve):
                link = linker(dve, dve_step)
                link(nc.vector.tensor_tensor(sq[:], y, y, ALU.mult))
                link(nc.vector.tensor_reduce(ss[:, 0, :], sq[:], AXX, ALU.add))
                nc.vector.tensor_scalar(ss[:, 1, :], ss[:, 0, :], 1.0 / P, EPS, ALU.mult, ALU.add
                                        ).then_inc(ms_ready, 1)
                dve.wait_ge(gain_in, 16)
                link(nc.vector.tensor_tensor(y, y, gain[:, None, :].to_broadcast([P, N, P]), ALU.mult))
                link(nc.vector.tensor_tensor(y, y, zs[:, first:].rearrange("p t (h n) -> p (t h) n", h=H), ALU.mult))
                dve.wait_ge(root_ready, 1)
                link(nc.vector.reciprocal(ss[:, 1, :], ss[:, 0, :]))
                nc.vector.tensor_tensor(y, y, ss[:, 1, :][:, :, None].to_broadcast([P, N, P]), ALU.mult
                                        ).then_inc(y_ready, 1)

            @block.scalar
            def _(act):
                act.wait_ge(ms_ready, 1)
                nc.scalar.activation(ss[:, 0, :], ss[:, 1, :], ACT.Sqrt).then_inc(root_ready, 1)
                for t in range(first, NT):
                    act.wait_ge(turned, t - first + 1)
                    nc.scalar.activation(mixT[:, 0:H, t * P:(t + 1) * P],
                                         ps[:, t % 4, :].rearrange("p (h n) -> p h n", h=H), ACT.Copy
                                         ).then_inc(copied, 1)

            @block.tensor
            def _(pe):
                pe.wait_ge(y_ready, 1)
                for t in range(first, NT):
                    if t - first >= 4:
                        pe.wait_ge(copied, t - first - 3)
                    for h in range(H):
                        last = nc.tensor.transpose(ps[:, t % 4, h * P:(h + 1) * P], o[:, t, h, :], kit.c("ident"))
                    last.then_inc(turned, 1)


def mix_out(nc, kit, L, tiles, mixT, w, w_arrived):
    with ExitStack() as mem, phase(nc, kit, "gates_in", "x0", "x1", "prod_ready", "gated", "sum_ready",
                                   "stored0", "stored1") as (
            gates_in, x0, x1, prod_ready, gated, sum_ready, stored0, stored1):
        x_in, stored = [x0, x1], [stored0, stored1]
        sb = lambda n, s: mem.enter_context(nc.sbuf_tensor(f"mo{n}_{L}", s, FP32))
        xb = sb("x", [P, 2, 2, 512])
        yb = sb("y", [P, 2, 2, 512])
        ps = kit.ps

        gates = sb("gates", [P, 2, D])

        def store(sp, i):
            t = tiles[i]
            sp.wait_ge(sum_ready, 2 * (i + 1))
            sp.dma_start(kit.x_d[t * P:(t + 1) * P, :], xb[:, i % 2].rearrange("p a n -> p (a n)")
                         ).then_inc(stored[i % 2], 16)

        with nc.Block() as block:
            @block.sync
            def _(sp):
                for g in range(2):
                    sp.dma_start(gates[:, g, :], mod_row(kit, g, 2)).then_inc(gates_in, 16)
                for i, t in enumerate(tiles):
                    b = i % 2
                    rows = kit.x_d[t * P:(t + 1) * P, :]
                    if i >= 2:
                        sp.wait_ge(stored[b], 16 * (i // 2))
                    sp.dma_start(xb[:, b].rearrange("p a n -> p (a n)"), rows).then_inc(x_in[b], 16)
                    if i >= 1:
                        store(sp, i - 1)
                store(sp, len(tiles) - 1)
                for b in range(2):
                    sp.wait_ge(stored[b], 16 * ((len(tiles) + 1 - b) // 2))

            @block.tensor
            def _(pe):
                pe.wait_ge(w_arrived, 16)
                for i, t in enumerate(tiles):
                    for half in range(2):
                        q = 2 * i + half
                        if q >= 4:
                            pe.wait_ge(gated, q - 3)
                        for k in range(KD):
                            last = nc.tensor.matmul(ps[:, q % 4, :], mixT[:, k, t * P:(t + 1) * P],
                                                    w[:, k, half * 512:(half + 1) * 512], start=k == 0,
                                                    stop=k == KD - 1)
                        last.then_inc(prod_ready, 1)

            @block.vector
            def _(dve):
                dve.wait_ge(gates_in, 32)
                for i, t in enumerate(tiles):
                    s = int(t >= NC)
                    dve.wait_ge(x_in[i % 2], 16 * (i // 2 + 1))
                    for half in range(2):
                        q = 2 * i + half
                        dve.wait_ge(prod_ready, q + 1)
                        nc.vector.tensor_tensor(yb[:, i % 2, half, :], ps[:, q % 4, :],
                                                gates[:, s, half * 512:(half + 1) * 512], ALU.mult
                                                ).then_inc(gated, 1)
                        dve.wait_ge(gated, q + 1)
                        nc.vector.tensor_tensor(xb[:, i % 2, half, :], xb[:, i % 2, half, :],
                                                yb[:, i % 2, half, :], ALU.add).then_inc(sum_ready, 1)


def peer_tables(nc, kit, L, tiles, keysT):
    with ExitStack() as mem, phase(nc, kit, "keys_in", "rows_in", "turned", "copied", "scale_ready",
                                   "stored") as (keys_in, rows_in, turned, copied, scale_ready, stored):
        sb = lambda n, s: mem.enter_context(nc.sbuf_tensor(f"pt{n}_{L}", s, FP32))
        keys = sb("keys", [P, HP, P])
        gain = sb("gain", [2, D])
        sc = sb("sc", [2, D])
        ps = kit.ps

        with nc.Block() as block:
            @block.sync
            def _(sp):
                sp.dma_start(sc[:], kit.mod_d[:, 4 * D:5 * D]).then_inc(rows_in, 16)
                sp.dma_start(gain[:], kit.norm2[L:L + 1, :].broadcast_to([2, D])).then_inc(rows_in, 16)
                sp.dma_start(keys[:], kit.peer_keys[L].rearrange("h s k d -> k (h s) d")).then_inc(keys_in, 16)
                for t in tiles:
                    s = int(t >= NC)
                    sp.dma_start(kit.rows_d[t, 1:2, :], kit.mod_d[s:s + 1, 3 * D:4 * D]).then_inc(stored, 16)
                    sp.dma_start(kit.rows_d[t, 2:3, :], kit.mod_d[s:s + 1, 5 * D:6 * D]).then_inc(stored, 16)
                sp.wait_ge(scale_ready, 1)
                for t in tiles:
                    s = int(t >= NC)
                    sp.dma_start(kit.rows_d[t, 0:1, :], sc[s:s + 1, :]).then_inc(stored, 16)
                sp.wait_ge(stored, 48 * len(tiles))

            @block.vector
            def _(dve):
                dve.wait_ge(rows_in, 32)
                nc.vector.scalar_tensor_tensor(out=sc[:], in0=sc[:], scalar=1.0, in1=gain[:], op0=ALU.add,
                                               op1=ALU.mult).then_inc(scale_ready, 1)

            @block.tensor
            def _(pe):
                pe.wait_ge(keys_in, 16)
                for q in range(HP // 4):
                    for i in range(4):
                        last = nc.tensor.transpose(ps[:, q, i * P:(i + 1) * P], keys[:, 4 * q + i, :],
                                                   kit.c("ident"))
                    last.then_inc(turned, 1)

            @block.scalar
            def _(act):
                for q in range(HP // 4):
                    act.wait_ge(turned, q + 1)
                    nc.scalar.activation(keysT[:, 4 * q:4 * q + 4, :].rearrange("p h n -> p (h n)"), ps[:, q, :],
                                         ACT.Copy).then_inc(copied, 1)


def peer_tile(nc, kit, L, m, cur, nxt, x_saved, wq_in=None):
    GROUP = 4
    LAG = 9
    NG = SLOTS // GROUP
    RING = kit.ring
    DG = 4
    H_AT = 4
    Q_AT, Q_STEP = 18, 5
    C_AT = Q_AT + (HP + 1) * Q_STEP + 3
    u_tab = kit.peer_u.rearrange("l e d -> (l e) d")
    v_tab = kit.peer_v.rearrange("l e d -> (l e) d")
    names = (["u%d" % i for i in range(RING)] + ["v%d" % i for i in range(RING)]
             + ["u_used", "gelu_ready", "coef_ready", "diag_ready", "v_used", "xg_in", "y_gated", "x_ready",
                "row_in", "ss_ready", "ms_ready", "root_ready", "h_ready", "h_turned", "hT_ready",
                "q_ready", "q_copied", "s_ready", "s_copied", "picked", "top_ready", "soft_ready", "eid_ready",
                "shifted", "dve_step"])
    with phase(nc, kit, *names, gathers=2 * RING) as sems:
        u_in, v_in = sems[:RING], sems[RING:2 * RING]
        (u_used, gelu_ready, coef_ready, diag_ready, v_used, xg_in, y_gated, x_ready, row_in, ss_ready,
         ms_ready, root_ready, h_ready, h_turned, hT_ready, q_ready, q_copied, s_ready, s_copied, picked,
         top_ready, soft_ready, eid_ready, shifted, dve_step) = sems[2 * RING:]
        ps = kit.ps
        ident = kit.c("ident")
        row = lambda ap, t: ap[bass.ds(t, 1), :, :].rearrange("a p n -> p (a n)")
        x_t = kit.x_d.rearrange("(t p) n -> t p n", p=P)
        pair_at = lambda k, first: (k - first) // Q_STEP if k >= first and (k - first) % Q_STEP == 0 else -1

        with nc.Block() as block:
            @block.sync
            def _(sp):
                if nxt is not None:
                    sp.dma_start(m.xn[:], row(x_t, nxt)).then_inc(row_in, 16)
                    for i in range(2):
                        sp.dma_start(m.mod[:, i, :], kit.rows_d[bass.ds(nxt, 1), i, :].broadcast_to([P, D])
                                     ).then_inc(row_in, 16)
                if cur is None:
                    sp.dma_start(m.xc[:], row(x_t, nxt)).then_inc(x_saved, 16)
                else:
                    sp.wait_ge(x_saved, 16)
                    sp.sem_clear(x_saved)
                    sp.dma_start(m.xc[:], row(x_t, cur)).then_inc(xg_in, 16)
                    sp.dma_start(m.gate_c[:], kit.rows_d[bass.ds(cur, 1), 2, :].broadcast_to([P, D])
                                 ).then_inc(xg_in, 16)
                    sp.wait_ge(x_ready, 1)
                    sp.dma_start(row(x_t, cur), m.xc[:]).then_inc(x_saved, 16)

            @block.gpsimd
            def _(pool):
                if cur is None:
                    return
                for k in range(SLOTS + LAG):
                    if k < SLOTS:
                        if k >= RING:
                            pool.wait_ge(u_used, k - RING + 1)
                        nc.gpsimd.indirect_dma_start(
                            m.ub[:, k % RING, :], None, u_tab,
                            bass.IndirectOffsetOnAxis(m.eid[:, k:k + 1], 0)).then_inc(u_in[k % RING], 16)
                    if k >= LAG:
                        kv = k - LAG
                        if kv >= RING:
                            pool.wait_ge(v_used, kv - RING + 1)
                        nc.gpsimd.indirect_dma_start(
                            m.vb[:, kv % RING, :], None, v_tab,
                            bass.IndirectOffsetOnAxis(m.eid[:, kv:kv + 1], 0)).then_inc(v_in[kv % RING], 16)
                for r in range(RING):
                    pool.wait_ge(u_in[r], 16 * ((SLOTS + RING - 1 - r) // RING))
                    pool.wait_ge(v_in[r], 16 * ((SLOTS + RING - 1 - r) // RING))

            @block.vector
            def _(dve):
                link = linker(dve, dve_step)

                def dot(k):
                    dve.wait_ge(u_in[k % RING], 16 * (k // RING + 1))
                    if k:
                        dve.wait_ge(u_used, k)
                    nc.vector.tensor_tensor_reduce(out=m.dot[:], in0=m.ub[:, k % RING, :], in1=m.hc[:],
                                                   scale=1.0, scalar=0.0, op0=ALU.mult, op1=ALU.add,
                                                   accum_out=m.act[:, k:k + 1]).then_inc(u_used, 1)

                def coefficients(g):
                    G = slice(g * GROUP, (g + 1) * GROUP)
                    dve.wait_ge(gelu_ready, g + 1)
                    nc.vector.tensor_tensor(m.coef[:, G], m.coef[:, G], m.gw[:, G], ALU.mult
                                            ).then_inc(coef_ready, 1)

                def norm():
                    dve.wait_ge(ss_ready, 1)
                    nc.vector.tensor_scalar(m.ss[:, 1:2], m.ss[:, 0:1], 1.0 / D, EPS, ALU.mult, ALU.add
                                            ).then_inc(ms_ready, 1)

                def modulate():
                    dve.wait_ge(root_ready, 1)
                    link(nc.vector.reciprocal(m.ss[:, 3:4], m.ss[:, 2:3]))
                    dve.wait_ge(row_in, 48)
                    link(nc.vector.scalar_tensor_tensor(out=m.hn[:], in0=m.xn[:], scalar=m.ss[:, 3:4],
                                                        in1=m.mod[:, 0, :], op0=ALU.mult, op1=ALU.mult))
                    nc.vector.tensor_tensor(m.hn[:], m.hn[:], m.mod[:, 1, :], ALU.add).then_inc(h_ready, 1)

                def top16(val, idx, src, rest):
                    link(nc.vector.max(val[:, 0:8], src))
                    link(nc.vector.max_index(idx[:, 0:8], val[:, 0:8], src))
                    link(nc.vector.match_replace(rest, val[:, 0:8], src, NEG))
                    link(nc.vector.max(val[:, 8:16], rest))
                    return nc.vector.max_index(idx[:, 8:16], val[:, 8:16], rest)

                def pick(q):
                    dve.wait_ge(s_copied, q + 1)
                    top16(m.sv[:, q, :], m.si[:, q, :], m.s[:, q % 4, :], m.rest[:, 0:NKEYS]).then_inc(picked, 1)
                    dve.wait_ge(picked, q + 1)
                    link(nc.vector.tensor_copy(m.sif[:, q, :], m.si[:, q, :]))

                def combine(h):
                    a = m.sv[:, 2 * h, :][:, :, None].to_broadcast([P, TOPK, TOPK])
                    b = m.sv[:, 2 * h + 1, :][:, None, :].to_broadcast([P, TOPK, TOPK])
                    link(nc.vector.tensor_tensor(m.cand[:].rearrange("p (a b) -> p a b", a=TOPK), a, b, ALU.add))
                    link(top16(m.fv[:, h, :], m.fi[:, h, :], m.cand[:], m.rest[:]))

                def less_max():
                    nc.vector.tensor_tensor(m.gn[:], m.fv[:], m.fv[:, :, 0:1].to_broadcast([P, PH, TOPK]),
                                            ALU.subtract).then_inc(top_ready, 1)

                def softmax():
                    dve.wait_ge(soft_ready, 1)
                    link(nc.vector.tensor_reduce(m.gsum[:, 0, :], m.gn[:], AXX, ALU.add))
                    link(nc.vector.reciprocal(m.gsum[:, 1, :], m.gsum[:, 0, :]))
                    link(nc.vector.tensor_tensor(m.gn[:], m.gn[:],
                                                 m.gsum[:, 1, :][:, :, None].to_broadcast([P, PH, TOPK]), ALU.mult))

                fi = m.fi[:].rearrange("p h k -> p (h k)")
                eq = m.eq[:].rearrange("p (a b) -> p a b", b=TOPK)

                def place(side):
                    op, by = ((ALU.logical_shift_right, 4), (ALU.bitwise_and, 15))[side]
                    link(nc.vector.tensor_scalar(m.place[:], fi, by, None, op))
                    link(nc.vector.tensor_copy(m.placef[:], m.place[:]))
                    link(nc.vector.tensor_tensor(eq, m.placef[:, :, None].to_broadcast([P, SLOTS, TOPK]),
                                                 kit.iota[:, None, :].to_broadcast([P, SLOTS, TOPK]),
                                                 ALU.is_equal))

                def key_there(side):
                    eq4 = m.eq[:].rearrange("p (h a b) -> p h a b", a=TOPK, b=TOPK)
                    key = m.sif[:].rearrange("p (h s) k -> p h s k", s=2)[:, :, side, :]
                    link(nc.vector.tensor_tensor(eq4, eq4, key[:, :, None, :].to_broadcast([P, PH, TOPK, TOPK]),
                                                 ALU.mult))

                def key_number(side):
                    link(nc.vector.tensor_reduce(m.num[:, side, :], eq, AXX, ALU.add))

                def expert_number():
                    link(nc.vector.tensor_scalar(m.num[:, 0, :], m.num[:, 0, :], float(NKEYS),
                                                 float(L * NKEYS * NKEYS), ALU.mult, ALU.add))
                    nc.vector.tensor_tensor(m.num[:, 0, :], m.num[:, 0, :], m.num[:, 1, :], ALU.add
                                            ).then_inc(eid_ready, 1)
                    dve.wait_ge(eid_ready, 1)

                def piece(k):
                    if k == H_AT:
                        norm()
                    elif k == H_AT + 2:
                        modulate()
                    q = pair_at(k, Q_AT + 2 * Q_STEP - 1)
                    if 0 <= q < HP:
                        pick(q)
                    c = k - C_AT
                    if 0 <= c < PH:
                        combine(c)
                    elif c == PH:
                        less_max()
                        place(0)
                    elif c == PH + 1:
                        key_there(0)
                    elif c == PH + 2:
                        key_number(0)
                        softmax()
                    elif c == PH + 3:
                        place(1)
                    elif c == PH + 4:
                        key_there(1)
                    elif c == PH + 5:
                        key_number(1)
                        expert_number()

                for k in range(SLOTS + LAG):
                    if cur is not None and k < SLOTS:
                        dot(k)
                        if k % GROUP == 2 and k > GROUP:
                            coefficients(k // GROUP - 1)
                    if cur is not None and k == SLOTS:
                        coefficients(NG - 1)
                    if nxt is not None:
                        piece(k)
                if nxt is not None:
                    dve.wait_ge(h_turned, 1)
                    if cur is not None:
                        dve.wait_ge(u_used, SLOTS)
                        dve.wait_ge(coef_ready, NG)
                    nc.vector.tensor_copy(m.hc[:], m.hn[:]).then_inc(shifted, 1)
                    nc.vector.tensor_copy(m.gw[:], m.gn[:].rearrange("p h k -> p (h k)")).then_inc(shifted, 1)
                if cur is not None:
                    dve.wait_ge(v_used, SLOTS)
                    dve.wait_ge(xg_in, 32)
                    nc.vector.tensor_tensor(m.dot[:], m.gate_c[:], ps[:, 0:2, :].rearrange("p b n -> p (b n)"),
                                            ALU.mult).then_inc(y_gated, 1)
                    dve.wait_ge(y_gated, 1)
                    nc.vector.tensor_tensor(m.xc[:], m.xc[:], m.dot[:], ALU.add).then_inc(x_ready, 1)
                if nxt is not None:
                    nc.vector.tensor_copy(m.eid[:], m.num[:, 0, :]).then_inc(shifted, 1)
                    dve.wait_ge(shifted, 3)

            @block.scalar
            def _(act):
                def diagonal(k):
                    act.wait_ge(coef_ready, k // GROUP + 1)
                    if k >= DG:
                        act.wait_ge(v_used, k - DG + 1)
                    nc.scalar.activation(m.diag[:, k % DG, :], ident, ACT.Copy, scale=m.coef[:, k:k + 1]
                                         ).then_inc(diag_ready, 1)

                def gelu(g):
                    act.wait_ge(u_used, (g + 1) * GROUP)
                    nc.scalar.activation(m.coef[:, g * GROUP:(g + 1) * GROUP],
                                         m.act[:, g * GROUP:(g + 1) * GROUP], ACT.Gelu_apprx_tanh
                                         ).then_inc(gelu_ready, 1)

                def scores_copy(q):
                    act.wait_ge(s_ready, q + 1)
                    if q >= 4:
                        act.wait_ge(picked, q - 3)
                    nc.scalar.activation(m.s[:, q % 4, :], ps[:, 6 + q % 2, 0:P], ACT.Copy).then_inc(s_copied, 1)

                def piece(k):
                    if k == H_AT:
                        act.wait_ge(row_in, 48)
                        nc.scalar.activation(m.hn[:], m.xn[:], ACT.Square, accum_out=m.ss[:, 0:1]
                                             ).then_inc(ss_ready, 1)
                        act.wait_ge(ms_ready, 1)
                        nc.scalar.activation(m.ss[:, 2:3], m.ss[:, 1:2], ACT.Sqrt).then_inc(root_ready, 1)
                    elif k == H_AT + 6:
                        act.wait_ge(h_turned, 1)
                        nc.scalar.activation(m.hT[:].rearrange("p k n -> p (k n)"),
                                             ps[:, 2:4, :].rearrange("p b n -> p (b n)"), ACT.Copy
                                             ).then_inc(hT_ready, 1)
                    q = pair_at(k, Q_AT)
                    if 0 <= q < HP:
                        act.wait_ge(q_ready, q + 1)
                        nc.scalar.activation(m.q[:, q % 2, :], ps[:, 4 + q % 2, 0:P], ACT.Copy).then_inc(q_copied, 1)
                    if 1 <= q <= HP:
                        scores_copy(q - 1)
                    if k == C_AT + PH:
                        act.wait_ge(top_ready, 1)
                        nc.scalar.activation(m.gn[:], m.gn[:], ACT.Exp).then_inc(soft_ready, 1)

                for k in range(SLOTS + LAG):
                    if cur is not None:
                        if k % GROUP == 0 and 0 < k <= SLOTS:
                            gelu(k // GROUP - 1)
                        if k >= LAG:
                            diagonal(k - LAG)
                    if nxt is not None:
                        piece(k)

            @block.tensor
            def _(pe):
                def add_row(k):
                    pe.wait_ge(v_in[k % RING], 16 * (k // RING + 1))
                    pe.wait_ge(diag_ready, k + 1)
                    for half in range(2):
                        last = nc.tensor.matmul(ps[:, half, :], m.diag[:, k % DG, :],
                                                m.vb[:, k % RING, half * 512:(half + 1) * 512],
                                                start=k == 0, stop=k == SLOTS - 1)
                    last.then_inc(v_used, 1)

                def piece(k):
                    if k == H_AT + 4:
                        pe.wait_ge(h_ready, 1)
                        for i in range(KD):
                            last = nc.tensor.transpose(ps[:, 2 + i // 4, (i % 4) * P:(i % 4 + 1) * P],
                                                       m.hn[:, i * P:(i + 1) * P], ident)
                        last.then_inc(h_turned, 1)
                    q = pair_at(k, Q_AT)
                    if 0 <= q < HP:
                        if q == 0:
                            pe.wait_ge(hT_ready, 1)
                            if wq_in is not None:
                                pe.wait_ge(wq_in, 32)
                        if q >= 2:
                            pe.wait_ge(q_copied, q - 1)
                        for i in range(KD):
                            last = nc.tensor.matmul(ps[:, 4 + q % 2, 0:P], m.wq[:, i, q * P:(q + 1) * P],
                                                    m.hT[:, i, :], start=i == 0, stop=i == KD - 1)
                        last.then_inc(q_ready, 1)
                    if 1 <= q <= HP:
                        pe.wait_ge(q_copied, q)
                        if q >= 3:
                            pe.wait_ge(s_copied, q - 2)
                        nc.tensor.matmul(ps[:, 6 + (q - 1) % 2, 0:P], m.q[:, (q - 1) % 2, :], m.keysT[:, q - 1, :],
                                         start=True, stop=True).then_inc(s_ready, 1)

                for k in range(SLOTS + LAG):
                    if cur is not None and k >= LAG:
                        add_row(k - LAG)
                    if nxt is not None:
                        piece(k)


def peer(nc, kit, L, first, wq_in):
    with ExitStack() as mem:
        sb = lambda n, s, t=FP32: mem.enter_context(nc.sbuf_tensor(f"pe{n}_{L}", s, t))
        m = Kit()
        m.wq = kit.wq
        m.keysT = sb("keysT", [P, HP, P])
        peer_tables(nc, kit, L, range(first, NT), m.keysT)
        m.hc, m.xc, m.gate_c = sb("hc", [P, D]), sb("xc", [P, D]), sb("gc", [P, D])
        m.eid, m.gw = sb("eid", [P, SLOTS], U32), sb("gw", [P, SLOTS])
        m.ub, m.vb = sb("ub", [P, kit.ring, D]), sb("vb", [P, kit.ring, D])
        m.dot, m.act, m.coef = sb("dot", [P, D]), sb("act", [P, SLOTS]), sb("coef", [P, SLOTS])
        m.diag = sb("diag", [P, 4, P])
        m.xn, m.hn, m.mod = sb("xn", [P, D]), sb("hn", [P, D]), sb("mod", [P, 2, D])
        m.ss, m.hT = sb("ss", [P, 4]), sb("hT", [P, KD, P])
        m.q, m.s = sb("q", [P, 2, P]), sb("s", [P, 4, P])
        m.sv, m.sif = sb("sv", [P, HP, TOPK]), sb("sif", [P, HP, TOPK])
        m.rest, m.cand = sb("rest", [P, TOPK * TOPK]), sb("cand", [P, TOPK * TOPK])
        m.fv, m.gn, m.gsum = sb("fv", [P, PH, TOPK]), sb("gn", [P, PH, TOPK]), sb("gsum", [P, 2, PH])
        m.placef, m.eq, m.num = sb("placef", [P, SLOTS]), sb("eq", [P, SLOTS * TOPK]), sb("num", [P, 2, SLOTS])
        m.si = sb("si", [P, HP, TOPK], U32)
        m.fi = sb("fi", [P, PH, TOPK], U32)
        m.place = sb("place", [P, SLOTS], U32)
        x_saved = mem.enter_context(nc.semaphore(f"x_saved_{L}"))
        peer_tile(nc, kit, L, m, None, first, x_saved, wq_in)
        with nc.Fori(first, NT - 1) as t:
            peer_tile(nc, kit, L, m, t, t + 1, x_saved)
        peer_tile(nc, kit, L, m, NT - 1, None, x_saved)
        nc.sync.wait_ge(x_saved, 16)
        nc.sync.sem_clear(x_saved)
        nc.sync.sem_clear(wq_in)
        nc.all_engine_barrier()


def final_norm(nc, kit):
    N = NT - NC
    with ExitStack() as mem, phase(nc, kit, "gain_in", "x_in", "ss_ready", "ms_ready", "root_ready", "y_ready",
                                   "stored", "dve_step") as (
            gain_in, x_in, ss_ready, ms_ready, root_ready, y_ready, stored, dve_step):
        sb = lambda n, s: mem.enter_context(nc.sbuf_tensor(f"fn{n}", s, FP32))
        gain = sb("gain", [P, D])
        x = sb("x", [P, N, D])
        sq = sb("sq", [P, D])
        ss = sb("ss", [P, 2, N])

        with nc.Block() as block:
            @block.sync
            def _(sp):
                sp.dma_start(x[:], kit.x_d[CTX:T, :].rearrange("(t p) n -> p t n", p=P)).then_inc(x_in, 16)
                sp.dma_start(gain[:], kit.final_norm.rearrange("(a n) -> a n", a=1).broadcast_to([P, D])
                             ).then_inc(gain_in, 16)
                for t in range(N):
                    sp.wait_ge(y_ready, t + 1)
                    sp.dma_start(kit.out[0, t * P:(t + 1) * P, :], x[:, t, :]).then_inc(stored, 16)
                sp.wait_ge(stored, 16 * N)

            @block.scalar
            def _(act):
                act.wait_ge(x_in, 16)
                for t in range(N):
                    if t:
                        act.wait_ge(ss_ready, t)
                    nc.scalar.activation(sq[:], x[:, t, :], ACT.Square, accum_out=ss[:, 0, t:t + 1]
                                         ).then_inc(ss_ready, 1)
                act.wait_ge(ms_ready, 1)
                nc.scalar.activation(ss[:, 0, :], ss[:, 1, :], ACT.Sqrt).then_inc(root_ready, 1)

            @block.vector
            def _(dve):
                link = linker(dve, dve_step)
                dve.wait_ge(ss_ready, N)
                nc.vector.tensor_scalar(ss[:, 1, :], ss[:, 0, :], 1.0 / D, EPS, ALU.mult, ALU.add
                                        ).then_inc(ms_ready, 1)
                dve.wait_ge(gain_in, 16)
                dve.wait_ge(root_ready, 1)
                link(nc.vector.reciprocal(ss[:, 1, :], ss[:, 0, :]))
                for t in range(N):
                    nc.vector.scalar_tensor_tensor(out=x[:, t, :], in0=x[:, t, :], scalar=ss[:, 1, t:t + 1],
                                                   in1=gain[:], op0=ALU.mult, op1=ALU.mult).then_inc(y_ready, 1)


def backbone(nc, kit, layers=range(DEPTH)):
    kit.phases = 0
    kit.ring = 6
    with ExitStack() as mem:
        sb = lambda n, s, t=FP32: mem.enter_context(nc.sbuf_tensor(n, s, t))
        kit.ps = mem.enter_context(nc.psum_tensor("ps", [P, 8, 512], FP32))
        kit.arena = sb("arena", [P, KD * HP * P])
        kit.wq = kit.arena[:, :].rearrange("p (k n) -> p k n", k=KD)
        kit.cst = sb("cst", [P, len(CONSTS) * P + TOPK])
        kit.iota = kit.cst[:, len(CONSTS) * P:]
        kit.eps = sb("eps", [P, 2])
        kit.prm = sb("prm", [P, NPRM])
        kit.x_d = nc.dram_tensor("x_rows", [T, D], FP32, kind="Internal").ap()
        kit.mod_d = nc.dram_tensor("mod_rows", [2, 6 * D], FP32, kind="Internal").ap()
        kit.rows_d = nc.dram_tensor("peer_rows", [NT, 3, D], FP32, kind="Internal").ap()
        setup(nc, kit)
        for L in layers:
            last = L == DEPTH - 1
            first = NC if last else 0
            modulation(nc, kit, L)
            with ExitStack() as lay, nc.semaphore(f"w_out_in_{L}") as w_arrived, \
                    nc.semaphore(f"wq_in_{L}") as wq_in:
                sl = lambda n, s: lay.enter_context(nc.sbuf_tensor(f"{n}_{L}", s, FP32))
                hT = sl("hT", [P, KD, T])
                qkvT = sl("qkvT", [P, NQKV, T])
                zs = sl("zs", [P, NT, GW])
                ab = sl("ab", [P, NT, 4 * H])
                gate = sl("gate", [P, NT, 4 * H])
                norm_in(nc, kit, L, hT)
                with ExitStack() as cv:
                    sc = lambda n, s: cv.enter_context(nc.sbuf_tensor(f"{n}_{L}", s, FP32))
                    fT, acc = sc("fT", [P, 2, T]), sc("acc", [P, 2, T])
                    projection(nc, kit, L, first, hT, qkvT, zs, ab, fT, acc)
                    branches(nc, kit, L, first, fT, acc, hT, ab, gate)
                o = qkvT[:, 2 * H:3 * H, :].rearrange("p a b -> p (a b)").rearrange("p (t h n) -> p t h n", t=NT, h=H)
                with ExitStack() as gd:
                    sg = lambda n, s: gd.enter_context(nc.sbuf_tensor(f"{n}_{L}", s, FP32))
                    both = lambda at: kit.arena[:, at:at + 2 * NT * GW].rearrange(
                        "p (d t h n) -> p d t h n", d=2, t=NT, h=H)
                    u, wT = both(0), both(2 * NT * GW)
                    kt = kit.arena[:, 4 * NT * GW:5 * NT * GW].rearrange("p (t h n) -> p t h n", t=NT, h=H)
                    qkd = sg("qkd", [P, 2, NT, H, P])
                    dec = sg("dec", [P, NT, 2, 4, H])
                    gdn_tiles(nc, kit, L, qkvT, gate, kt, u, wT, qkd, dec)
                    gdn_scan(nc, kit, L, qkvT, kt, u, wT, qkd, dec, o)
                w_out = sl("w_out", [P, KD, D])
                gdn_out(nc, kit, L, first, o, zs, hT, w_out, w_arrived, wq_in)
                mix_out(nc, kit, L, list(range(first, NT)), hT, w_out, w_arrived)
                lay.close()
                peer(nc, kit, L, first, wq_in)
                nc.sync.sem_clear(w_arrived)
        final_norm(nc, kit)


def constants():
    import numpy as np

    i, j = np.arange(P)[:, None], np.arange(P)[None, :]
    same = i // CHUNK == j // CHUNK
    c = {"ident": i == j, "L0": same & (i <= j), "L1": same & (i >= j), "M0": same & (i > j),
         "M1": same & (i < j), "CH0": (i < CHUNK) & (j >= 0), "CH1": (i >= CHUNK) & (j >= 0),
         "ones": np.ones((P, P)), "gmean": (i // 64 == j // 64) / 64.0}
    ang = 2 * np.pi * ((i % 64) * (j % 64) % 64) / 64
    c["C64"], c["S64"] = (i // 64 == j // 64) * np.cos(ang), (i // 64 == j // 64) * np.sin(ang)
    for n, b in enumerate(LEVELS):
        pair = (i // (2 * b) == j // (2 * b))
        c[f"B0_{n}"], c[f"B1_{n}"] = pair & (i // b > j // b), pair & (i // b < j // b)
    cst = np.concatenate([np.asarray(c[k], np.float32) for k in CONSTS]
                         + [np.broadcast_to(np.arange(TOPK, dtype=np.float32), (P, TOPK))], axis=1)

    def dft(n):
        k = np.arange(n)
        a = 2 * np.pi * (np.outer(k, k) % n) / n
        s = 1 / np.sqrt(n * 64.0)
        return np.stack([np.cos(a) * s, -np.sin(a) * s]).astype(np.float32)

    return {"consts": np.ascontiguousarray(cst), "dft_l": dft(SEQ), "dft_c": dft(CTX)}


_INS = ["x", "c", "ctx", "c_ctx", "w_mod", "b_mod", "norm1", "norm2", "w_in", "conv_qkv", "a_log", "dt_bias",
        "gdn_norm", "dw_w", "dw_b", "gn_w", "gn_b", "w_out", "peer_wq", "peer_keys", "peer_u", "peer_v",
        "final_norm"]


def build(nc, a, out):
    kit = Kit()
    kit.x, kit.cnd, kit.ctx, kit.c_ctx = a["x"], a["c"], a["ctx"], a["c_ctx"]
    kit.w_mod, kit.b_mod, kit.norm1, kit.norm2 = a["w_mod"], a["b_mod"], a["norm1"], a["norm2"]
    kit.w_in, kit.conv_qkv, kit.a_log, kit.dt_bias = a["w_in"], a["conv_qkv"], a["a_log"], a["dt_bias"]
    kit.gdn_norm, kit.dw_w, kit.dw_b = a["gdn_norm"], a["dw_w"], a["dw_b"]
    kit.gn_w, kit.gn_b, kit.w_out = a["gn_w"], a["gn_b"], a["w_out"]
    kit.peer_wq, kit.peer_keys, kit.peer_u, kit.peer_v = a["peer_wq"], a["peer_keys"], a["peer_u"], a["peer_v"]
    kit.final_norm, kit.consts, kit.dft_l, kit.dft_c = a["final_norm"], a["consts"], a["dft_l"], a["dft_c"]
    kit.out = out
    backbone(nc, kit)


def kernel(**inputs):
    import numpy as _np
    import concourse.bacc as _bacc
    from concourse.bass_utils import run_bass_kernel_spmd as _run

    nc = _bacc.Bacc("TRN2", target_bir_lowering=False, num_devices=1)
    arrays, args = {}, {}
    for name, a in [(n, inputs[n]) for n in _INS] + list(constants().items()):
        a = _np.ascontiguousarray(a)
        arrays[f"in_{name}_dram"] = a
        args[name] = nc.dram_tensor(f"in_{name}_dram", a.shape, mybir.dt.from_np(a.dtype), kind="ExternalInput").ap()
    out = nc.dram_tensor("out_0_dram", (1, SEQ, D), FP32, kind="ExternalOutput").ap()
    build(nc, args, out)
    r = _run(nc, [arrays], core_ids=[0])
    return r.results[0]["out_0_dram"]
```
